# Optimizing a Trainium2 kernel written in Bass

```python
import math
import jax, jax.numpy as jnp
from jax import lax
import numpy as np

D_MODEL = 1024
BATCH = 1
SEQ = 2048
DEPTH = 1

D_MIX = D_MODEL
A_WIDTH = D_MIX // 2
A_GROUPS = 4
A_CH = A_WIDTH // A_GROUPS
CHUNK = 128
SB_WIDTH = D_MIX - A_WIDTH
SB_HEADS = 8
SB_HEAD_DIM = SB_WIDTH // SB_HEADS
QBLK = 128
IN_WIDTH = 2 * A_WIDTH + 3 * SB_WIDTH
MEM_LEN = 256
X_HEADS = 4
X_HEAD_DIM = D_MODEL // X_HEADS
N_GROUPS = 4
EXPERTS_PER_GROUP = 8
N_EXPERTS = N_GROUPS * EXPERTS_PER_GROUP
TOP_K = 2
D_EXPERT = D_MODEL // 2
MOE_BLOCK = 128
EPS = 1e-6

kernel_name = "hybrid_gmlp_stickbreak_hiermoe_trunk"

def rmsnorm(x, g):
    xf = x.astype(jnp.float32)
    y = xf * lax.rsqrt(jnp.mean(xf * xf, axis=-1, keepdims=True) + EPS)
    return (y * g.astype(jnp.float32)).astype(x.dtype)

def chunk_gmlp(u, v, v_gain, w_s, b_s):
    B, S = u.shape[0], u.shape[1]
    n_chunks = S // CHUNK
    u = jax.nn.gelu(u)
    v = rmsnorm(jax.nn.gelu(v), v_gain)
    vc = v.reshape(B, n_chunks, CHUNK, A_GROUPS, A_CH)
    mask = jnp.tril(jnp.ones((CHUNK, CHUNK), dtype=w_s.dtype))
    ws = w_s * mask[None]
    mixed = jnp.einsum('gts,bcsgd->bctgd', ws, vc) + b_s.T[None, None, :, :, None]
    return u * mixed.reshape(B, S, A_GROUPS, A_CH)

def stick_breaking_attention(q, k, v):
    B, S, H, Dh = q.shape
    nb = S // QBLK
    scale = 1.0 / math.sqrt(Dh)
    qb = q.reshape(B, nb, QBLK, H, Dh).transpose(1, 0, 3, 2, 4)
    kh = k.transpose(0, 2, 1, 3)
    vh = v.transpose(0, 2, 1, 3)
    key_pos = jnp.arange(S)

    def block(args):
        i, qi = args
        z = jnp.einsum('bhqd,bhkd->bhqk', qi, kh).astype(jnp.float32) * scale
        q_pos = i * QBLK + jnp.arange(QBLK)
        strict = key_pos[None, :] < q_pos[:, None]
        log_1mb = jnp.where(strict, jax.nn.log_sigmoid(-z), 0.0)
        after = lax.cumsum(log_1mb, axis=3, reverse=True) - log_1mb
        a = jnp.where(strict, jnp.exp(jax.nn.log_sigmoid(z) + after), 0.0)
        return jnp.einsum('bhqk,bhkd->bhqd', a.astype(vh.dtype), vh)

    out = lax.map(block, (jnp.arange(nb), qb))
    return out.transpose(1, 0, 3, 2, 4).reshape(B, S, H * Dh)

def memory_cross_attention(h, m, w_q, w_k, w_v, w_o):
    B, S, _ = h.shape
    M = m.shape[1]
    q = (h @ w_q).reshape(B, S, X_HEADS, X_HEAD_DIM)
    k = (m @ w_k).reshape(B, M, X_HEADS, X_HEAD_DIM)
    v = (m @ w_v).reshape(B, M, X_HEADS, X_HEAD_DIM)
    s = jnp.einsum('bshd,bmhd->bhsm', q, k).astype(jnp.float32) / math.sqrt(X_HEAD_DIM)
    p = jax.nn.softmax(s, axis=-1).astype(v.dtype)
    o = jnp.einsum('bhsm,bmhd->bshd', p, v).reshape(B, S, X_HEADS * X_HEAD_DIM)
    return o @ w_o

def hierarchical_moe(h, w_group, b_group, w_router, b_router, w1, w3, w2):
    B, S, D = h.shape
    t = h.reshape(-1, D)
    T = t.shape[0]
    g_logits = (t @ w_group).astype(jnp.float32) + b_group.astype(jnp.float32)
    p_group = jax.nn.softmax(g_logits, axis=-1)
    g_sel = jnp.argmax(g_logits, axis=-1)
    g_gate = jnp.take_along_axis(p_group, g_sel[:, None], axis=1)[:, 0]
    e_logits = ((t @ w_router).astype(jnp.float32) + b_router.astype(jnp.float32)).reshape(T, N_GROUPS, EXPERTS_PER_GROUP)
    e_sel_logits = jnp.take_along_axis(e_logits, g_sel[:, None, None], axis=1)[:, 0]
    top_v, top_i = lax.top_k(e_sel_logits, TOP_K)
    gates = g_gate[:, None] * jax.nn.softmax(top_v, axis=-1)
    eid = g_sel[:, None] * EXPERTS_PER_GROUP + top_i

    flat_e = eid.reshape(-1)
    N = T * TOP_K
    order = jnp.argsort(flat_e, stable=True)
    sorted_e = flat_e[order]
    counts = jnp.bincount(flat_e, length=N_EXPERTS)
    padded = ((counts + MOE_BLOCK - 1) // MOE_BLOCK) * MOE_BLOCK
    start = jnp.cumsum(counts) - counts
    pend = jnp.cumsum(padded)
    pstart = pend - padded
    dest = pstart[sorted_e] + (jnp.arange(N) - start[sorted_e])
    P = N + N_EXPERTS * MOE_BLOCK
    n_blocks = P // MOE_BLOCK
    buf = jnp.zeros((P, D), t.dtype).at[dest].set(t[order // TOP_K])
    blk_e = jnp.minimum(jnp.searchsorted(pend, jnp.arange(n_blocks) * MOE_BLOCK, side='right'), N_EXPERTS - 1)

    def expert_block(args):
        xb, e = args
        return (jax.nn.silu(xb @ w1[e]) * (xb @ w3[e])) @ w2[e]

    ybuf = lax.map(expert_block, (buf.reshape(n_blocks, MOE_BLOCK, D), blk_e)).reshape(P, D)
    y_assign = jnp.zeros((N, D), ybuf.dtype).at[order].set(ybuf[dest])
    y = jnp.einsum('tkd,tk->td', y_assign.reshape(T, TOP_K, D), gates.astype(ybuf.dtype))
    return y.reshape(B, S, D)

def setup_inputs(seed: int = 0) -> dict:
    key = jax.random.key(seed)
    ks = jax.random.split(key, 32)
    f32 = jnp.float32
    n = lambda k, shape, s: jax.random.normal(k, shape, f32) * s
    gain = lambda k, shape: 1.0 + 0.05 * jax.random.normal(k, shape, f32)
    L, D = DEPTH, D_MODEL
    return {
        "x": jax.random.normal(ks[0], (BATCH, SEQ, D), f32),
        "mem": jax.random.normal(ks[1], (BATCH, MEM_LEN, D), f32),
        "norm_mix": gain(ks[2], (L, D)),
        "w_in": n(ks[3], (L, D, IN_WIDTH), D ** -0.5),
        "v_norm": gain(ks[4], (L, A_GROUPS, A_CH)),
        "w_spatial": n(ks[5], (L, A_GROUPS, CHUNK, CHUNK), CHUNK ** -0.5),
        "b_spatial": gain(ks[6], (L, A_GROUPS, CHUNK)),
        "out_norm_a": gain(ks[7], (L, A_WIDTH)),
        "out_norm_b": gain(ks[8], (L, SB_WIDTH)),
        "w_out": n(ks[9], (L, D_MIX, D), D_MIX ** -0.5),
        "norm_cross": gain(ks[10], (L, D)),
        "norm_mem": gain(ks[11], (L, D)),
        "w_xq": n(ks[12], (L, D, D), D ** -0.5),
        "w_xk": n(ks[13], (L, D, D), D ** -0.5),
        "w_xv": n(ks[14], (L, D, D), D ** -0.5),
        "w_xo": n(ks[15], (L, D, D), D ** -0.5),
        "norm_moe": gain(ks[16], (L, D)),
        "w_group": n(ks[17], (L, D, N_GROUPS), D ** -0.5),
        "b_group": n(ks[18], (L, N_GROUPS), 0.01),
        "w_router": n(ks[19], (L, D, N_EXPERTS), D ** -0.5),
        "b_router": n(ks[20], (L, N_EXPERTS), 0.01),
        "w1": n(ks[21], (L, N_EXPERTS, D, D_EXPERT), D ** -0.5),
        "w3": n(ks[22], (L, N_EXPERTS, D, D_EXPERT), D ** -0.5),
        "w2": n(ks[23], (L, N_EXPERTS, D_EXPERT, D), D_EXPERT ** -0.5),
        "norm_final": gain(ks[24], (D,)),
    }

def reference(x, mem, norm_mix, w_in, v_norm, w_spatial, b_spatial, out_norm_a, out_norm_b, w_out,
              norm_cross, norm_mem, w_xq, w_xk, w_xv, w_xo, norm_moe, w_group, b_group, w_router,
              b_router, w1, w3, w2, norm_final):
    B, S, D = x.shape
    c1 = A_WIDTH
    c2 = 2 * A_WIDTH
    c3 = c2 + SB_WIDTH
    c4 = c3 + SB_WIDTH
    for l in range(DEPTH):
        h = rmsnorm(x, norm_mix[l])
        z = h @ w_in[l]
        u_a = z[..., :c1].reshape(B, S, A_GROUPS, A_CH)
        v_a = z[..., c1:c2].reshape(B, S, A_GROUPS, A_CH)
        q_b = z[..., c2:c3].reshape(B, S, SB_HEADS, SB_HEAD_DIM)
        k_b = z[..., c3:c4].reshape(B, S, SB_HEADS, SB_HEAD_DIM)
        v_b = z[..., c4:].reshape(B, S, SB_HEADS, SB_HEAD_DIM)
        y_a = chunk_gmlp(u_a, v_a, v_norm[l], w_spatial[l], b_spatial[l]).reshape(B, S, A_WIDTH)
        y_b = stick_breaking_attention(q_b, k_b, v_b)
        y = jnp.concatenate([rmsnorm(y_a, out_norm_a[l]), rmsnorm(y_b, out_norm_b[l])], axis=-1)
        x = x + y @ w_out[l]
        h = rmsnorm(x, norm_cross[l])
        m = rmsnorm(mem, norm_mem[l])
        x = x + memory_cross_attention(h, m, w_xq[l], w_xk[l], w_xv[l], w_xo[l])
        h = rmsnorm(x, norm_moe[l])
        x = x + hierarchical_moe(h, w_group[l], b_group[l], w_router[l], b_router[l], w1[l], w3[l], w2[l])
    return rmsnorm(x, norm_final)


_drawn_inputs = setup_inputs


def setup_inputs(seed=0):
    import zlib

    import numpy as np

    out = dict(_drawn_inputs(seed))
    spreads = {}
    factors = {'norm_cross': 5.245,
     'norm_mem': 4.79,
     'b_group': 33.108,
     'b_router': 33.081,
     'norm_moe': 5.006}
    for name, (base, spread) in spreads.items():
        noise = np.random.default_rng([zlib.crc32(name.encode()), seed]).standard_normal(out[name].shape)
        drawn = base * np.exp(spread * noise) if base else spread * noise
        out[name] = __import__('jax').numpy.asarray(drawn.astype(out[name].dtype))
    for name, factor in factors.items():
        out[name] = (out[name] * factor).astype(out[name].dtype)
    return out
```

```python
import numpy as np
import concourse.bass as bass
from concourse import mybir
from concourse.alu_op_type import AluOpType as ALU
from contextlib import ExitStack

ACT = mybir.ActivationFunctionType
AX = mybir.AxisListType
F32 = mybir.dt.float32
F32R = mybir.dt.float32r
BF16 = mybir.dt.bfloat16
I32 = mybir.dt.int32
U32 = mybir.dt.uint32

P = 128
BANK = 512
EPS = 1e-6


class Scope:

    def __init__(self, nc, stack, stage):
        self.nc, self.stack, self.stage, self.sems = nc, stack, stage, []
        stack.callback(self.close)

    def close(self):
        if self.sems:
            self.nc.clear_and_free_semaphores(self.sems)
            self.nc.all_engine_barrier()

    def sbuf(self, name, shape, dtype=F32):
        return self.stack.enter_context(self.nc.sbuf_tensor(f"{self.stage}_{name}", shape, dtype))

    def psum(self, name, shape, dtype=F32):
        return self.stack.enter_context(self.nc.psum_tensor(f"{self.stage}_{name}", shape, dtype))

    def sem(self, name):
        self.sems.append(self.nc.alloc_semaphore(f"{self.stage}_{name}"))
        return self.sems[-1]


def as_f32(tile):
    return tile.bitcast(F32)


def split_product(pe, out, left_hi, left_lo, right_hi, right_lo, first, last):
    pe.matmul(out, left_hi, right_hi, start=first, stop=False)
    pe.matmul(out, left_hi, right_lo, start=False, stop=False)
    return pe.matmul(out, left_lo, right_hi, start=False, stop=last)


def project_qkv(nc, x, gain, w_in, ident, half, qt, kt, v):
    tokens, width = x.shape
    tiles, rows = tokens // P, width // P
    first_col = w_in.shape[1] - 3 * BANK
    heads, head_dim = qt.shape[0], qt.shape[1] // 2
    cols = w_in.shape[1] - first_col
    with ExitStack() as stack:
        s = Scope(nc, stack, "qkv")
        w_hi = s.sbuf("w_hi", [P, rows, cols], F32R)
        w_lo = s.sbuf("w_lo", [P, rows, cols], F32R)
        w_raw = s.sbuf("w_raw", [P, 2, cols])
        gains = s.sbuf("gains", [P, width])
        xs = s.sbuf("xs", [P, 2, width])
        hs = s.sbuf("hs", [P, 2, width])
        junk = s.sbuf("junk", [P, width], BF16)
        stat = s.sbuf("stat", [P, 2, 4])
        h_hi = s.sbuf("h_hi", [P, 2, rows, P], F32R)
        h_lo = s.sbuf("h_lo", [P, 2, rows, P], F32R)
        q_parts = s.sbuf("q_parts", [P, heads, 2, head_dim], F32R)
        k_parts = s.sbuf("k_parts", [P, heads, 2, head_dim], F32R)
        q_t = s.sbuf("q_t", [P, 2, heads, P], F32R)
        k_t = s.sbuf("k_t", [P, 2, heads, P], F32R)
        v_out = s.sbuf("v_out", [P, 2, BANK])
        ht_ps = s.psum("ht_ps", [P, rows, P])
        z_ps = s.psum("z_ps", [P, 3, BANK])
        t_ps = s.psum("t_ps", [P, heads, P])

        w_loaded = [s.sem(f"w_loaded{i}") for i in range(2)]
        gains_loaded = s.sem("gains_loaded")
        w_hi_done, w_lo_done = s.sem("w_hi_done"), s.sem("w_lo_done")
        x_loaded = [s.sem(f"x_loaded{i}") for i in range(2)]
        squared, meaned, rooted, h_done = s.sem("squared"), s.sem("meaned"), s.sem("rooted"), s.sem("h_done")
        ht_done, hh_done, hl_done = s.sem("ht_done"), s.sem("hh_done"), s.sem("hl_done")
        zq_done, zk_done, zv_done = s.sem("zq_done"), s.sem("zk_done"), s.sem("zv_done")
        q_hi, q_lo, k_hi, k_lo = s.sem("q_hi"), s.sem("q_lo"), s.sem("k_hi"), s.sem("k_lo")
        qt_done, kt_done = s.sem("qt_done"), s.sem("kt_done")
        qt_act, qt_dve, kt_act, kt_dve = s.sem("qt_act"), s.sem("qt_dve"), s.sem("kt_act"), s.sem("kt_dve")
        v_done = s.sem("v_done")
        stored = [s.sem(f"stored{i}") for i in range(2)]
        half_heads = heads // 2

        with nc.Block() as block:
            @block.sync
            def _(sp):
                sp.dma_start(gains[:], gain.partition_broadcast(P)).then_inc(gains_loaded, 16)

                def load_x(t, slot):
                    sp.dma_start(xs[:, slot], x[bass.ds(t * P, P), :]).then_inc(x_loaded[slot], 16)

                load_x(0, 0)
                load_x(1, 1)
                for r in range(rows):
                    if r >= 2:
                        sp.wait_ge(w_lo_done, r - 1)
                    sp.dma_start(w_raw[:, r % 2], w_in[r * P:(r + 1) * P, first_col:]).then_inc(w_loaded[r % 2], 16)

                def store(t, slot):
                    sp.wait_ge(qt_act, t + 1)
                    sp.wait_ge(qt_dve, t + 1)
                    sp.dma_start(qt[:, :, bass.ds(t * P, P)].rearrange("h p t -> p h t"), as_f32(q_t[:, slot])).then_inc(stored[slot], 16)
                    sp.wait_ge(v_done, t + 1)
                    sp.dma_start(v[bass.ds(t * P, P), :], v_out[:, slot]).then_inc(stored[slot], 16)
                    sp.wait_ge(kt_act, t + 1)
                    sp.wait_ge(kt_dve, t + 1)
                    sp.dma_start(kt[:, :, bass.ds(t * P, P)].rearrange("h p t -> p h t"), as_f32(k_t[:, slot])).then_inc(stored[slot], 16)

                with sp.Fori(0, tiles // 2 - 1) as j:
                    for slot in range(2):
                        sp.wait_ge(h_done, 2 * j + slot + 1)
                        load_x(2 * j + slot + 2, slot)
                        store(2 * j + slot, slot)
                for slot in range(2):
                    store(tiles - 2 + slot, slot)
                for slot in range(2):
                    sp.wait_ge(stored[slot], 16 * 3 * tiles // 2)

            @block.gpsimd
            def _(pool):
                def root(t, slot):
                    pool.wait_ge(meaned, t + 1)
                    nc.gpsimd.tensor_tensor(stat[:, slot, 2:3], stat[:, slot, 1:2], half[:, 0:1], ALU.pow).then_inc(rooted, 1)

                root(0, 0)
                with pool.Fori(0, tiles // 2 - 1) as j:
                    root(2 * j + 1, 1)
                    root(2 * j + 2, 0)
                root(tiles - 1, 1)

            @block.scalar
            def _(act):
                def square(j, slot):
                    act.wait_ge(x_loaded[slot], 16 * (j + 1))
                    nc.scalar.activation(junk[:], xs[:, slot], ACT.Square, accum_out=stat[:, slot, 0:1]).then_inc(squared, 1)

                def high_h(t, slot):
                    act.wait_ge(ht_done, t + 1)
                    for part in range(2):
                        last = nc.scalar.copy(h_hi[:, slot, 4 * part:4 * part + 4], ht_ps[:, 4 * part:4 * part + 4])
                    last.then_inc(hh_done, 1)

                square(0, 0)
                for r in range(rows):
                    act.wait_ge(w_loaded[r % 2], 16 * (r // 2 + 1))
                    nc.scalar.copy(w_hi[:, r], w_raw[:, r % 2]).then_inc(w_hi_done, 1)
                high_h(0, 0)

                def tile(j, slot, last_tile=False):
                    t = 2 * j + slot
                    if not last_tile:
                        square(j + slot, 1 - slot)
                    act.wait_ge(zq_done, t + 1)
                    act.wait_ge(qt_done, t)
                    nc.scalar.activation(q_parts[:, :, 0, :], z_ps[:, 0].rearrange("p (h d) -> p h d", h=heads),
                                         ACT.Copy, scale=head_dim ** -0.5).then_inc(q_hi, 1)
                    act.wait_ge(zk_done, t + 1)
                    act.wait_ge(kt_done, t)
                    nc.scalar.copy(k_parts[:, :, 0, :], z_ps[:, 1].rearrange("p (h d) -> p h d", h=heads)).then_inc(k_hi, 1)
                    act.wait_ge(qt_done, t + 1)
                    act.wait_ge(stored[slot], 48 * j)
                    nc.scalar.copy(q_t[:, slot, 0:half_heads], t_ps[:, 0:half_heads]).then_inc(qt_act, 1)
                    act.wait_ge(zv_done, t + 1)
                    nc.scalar.copy(v_out[:, slot], z_ps[:, 2]).then_inc(v_done, 1)
                    if not last_tile:
                        high_h(t + 1, 1 - slot)
                    act.wait_ge(kt_done, t + 1)
                    nc.scalar.copy(k_t[:, slot, 0:half_heads], t_ps[:, 0:half_heads]).then_inc(kt_act, 1)

                with act.Fori(0, tiles // 2 - 1) as j:
                    tile(j, 0)
                    tile(j, 1)
                tile(tiles // 2 - 1, 0)
                tile(tiles // 2 - 1, 1, last_tile=True)

            @block.vector
            def _(dve):
                dve.wait_ge(gains_loaded, 16)

                def norm(t, slot):
                    dve.wait_ge(squared, t + 1)
                    nc.vector.tensor_scalar(stat[:, slot, 1:2], stat[:, slot, 0:1], 1.0 / width, EPS, ALU.mult, ALU.add).then_inc(meaned, 1)
                    dve.wait_ge(rooted, t + 1)
                    nc.vector.scalar_tensor_tensor(out=hs[:, slot], in0=xs[:, slot], scalar=stat[:, slot, 2:3], in1=gains[:],
                                                   op0=ALU.mult, op1=ALU.mult).then_inc(h_done, 1)

                def low_h(t, slot):
                    dve.wait_ge(hh_done, t + 1)
                    for part in range(2):
                        cut = slice(4 * part, 4 * part + 4)
                        last = nc.vector.tensor_tensor(h_lo[:, slot, cut], ht_ps[:, cut], as_f32(h_hi[:, slot, cut]), ALU.subtract)
                    last.then_inc(hl_done, 1)

                norm(0, 0)
                for r in range(rows):
                    dve.wait_ge(w_hi_done, r + 1)
                    nc.vector.tensor_tensor(w_lo[:, r], w_raw[:, r % 2], as_f32(w_hi[:, r]), ALU.subtract).then_inc(w_lo_done, 1)
                low_h(0, 0)

                def tile(j, slot, last_tile=False):
                    t = 2 * j + slot
                    if not last_tile:
                        norm(t + 1, 1 - slot)
                    dve.wait_ge(q_hi, t + 1)
                    nc.vector.scalar_tensor_tensor(out=q_parts[:, :, 1, :], in0=z_ps[:, 0].rearrange("p (h d) -> p h d", h=heads),
                                                   scalar=head_dim ** -0.5, in1=as_f32(q_parts[:, :, 0, :]),
                                                   op0=ALU.mult, op1=ALU.subtract).then_inc(q_lo, 1)
                    dve.wait_ge(k_hi, t + 1)
                    nc.vector.tensor_tensor(k_parts[:, :, 1, :], z_ps[:, 1].rearrange("p (h d) -> p h d", h=heads),
                                            as_f32(k_parts[:, :, 0, :]), ALU.subtract).then_inc(k_lo, 1)
                    dve.wait_ge(qt_done, t + 1)
                    dve.wait_ge(stored[slot], 48 * j)
                    nc.vector.tensor_copy(q_t[:, slot, half_heads:], t_ps[:, half_heads:]).then_inc(qt_dve, 1)
                    if not last_tile:
                        low_h(t + 1, 1 - slot)
                    dve.wait_ge(kt_done, t + 1)
                    nc.vector.tensor_copy(k_t[:, slot, half_heads:], t_ps[:, half_heads:]).then_inc(kt_dve, 1)

                with dve.Fori(0, tiles // 2 - 1) as j:
                    tile(j, 0)
                    tile(j, 1)
                tile(tiles // 2 - 1, 0)
                tile(tiles // 2 - 1, 1, last_tile=True)

            @block.tensor
            def _(pe):
                def transpose_h(t, slot):
                    pe.wait_ge(h_done, t + 1)
                    pe.wait_ge(hl_done, t)
                    for r in range(rows):
                        last = nc.tensor.transpose(ht_ps[:, r], hs[:, slot, r * P:(r + 1) * P], ident)
                    last.then_inc(ht_done, 1)

                def product(slot, chunk, done):
                    for r in range(rows):
                        last = split_product(nc.tensor, z_ps[:, chunk], h_hi[:, slot, r], h_lo[:, slot, r],
                                             w_hi[:, r, chunk * BANK:(chunk + 1) * BANK],
                                             w_lo[:, r, chunk * BANK:(chunk + 1) * BANK], r == 0, r == rows - 1)
                    last.then_inc(done, 1)

                transpose_h(0, 0)
                pe.wait_ge(w_lo_done, rows)

                def tile(j, slot, last_tile=False):
                    t = 2 * j + slot
                    pe.wait_ge(hl_done, t + 1)
                    pe.wait_ge(q_lo, t)
                    product(slot, 0, zq_done)
                    pe.wait_ge(k_lo, t)
                    product(slot, 1, zk_done)
                    pe.wait_ge(q_lo, t + 1)
                    pe.wait_ge(kt_act, t)
                    pe.wait_ge(kt_dve, t)
                    for h in range(heads):
                        last = nc.tensor.transpose(t_ps[:, h], as_f32(q_parts[:, h].rearrange("p a d -> p (a d)")), ident)
                    last.then_inc(qt_done, 1)
                    pe.wait_ge(v_done, t)
                    product(slot, 2, zv_done)
                    if not last_tile:
                        transpose_h(t + 1, 1 - slot)
                    pe.wait_ge(k_lo, t + 1)
                    pe.wait_ge(qt_act, t + 1)
                    pe.wait_ge(qt_dve, t + 1)
                    for h in range(heads):
                        last = nc.tensor.transpose(t_ps[:, h], as_f32(k_parts[:, h].rearrange("p a d -> p (a d)")), ident)
                    last.then_inc(kt_done, 1)

                with pe.Fori(0, tiles // 2 - 1) as j:
                    tile(j, 0)
                    tile(j, 1)
                tile(tiles // 2 - 1, 0)
                tile(tiles // 2 - 1, 1, last_tile=True)


def mix_chunks(nc, x, gain, w_in, v_gain, w_spatial, b_spatial, out_gain, ident, half, ya):
    tokens, width = x.shape
    tiles, rows = tokens // P, width // P
    groups, chan = v_gain.shape
    cols = 2 * BANK
    with ExitStack() as stack:
        s = Scope(nc, stack, "gmlp")
        w_hi = s.sbuf("w_hi", [P, rows, cols], F32R)
        w_lo = s.sbuf("w_lo", [P, rows, cols], F32R)
        w_raw = s.sbuf("w_raw", [P, 2, cols])
        gains = s.sbuf("gains", [P, width])
        v_gains = s.sbuf("v_gains", [P, BANK])
        out_gains = s.sbuf("out_gains", [P, BANK])
        ws_raw = s.sbuf("ws_raw", [P, groups, P])
        ws_t = s.sbuf("ws_t", [P, groups, P])
        bias = s.sbuf("bias", [P, groups])
        xs = s.sbuf("xs", [P, 2, width])
        hs = s.sbuf("hs", [P, 2, width])
        junk = s.sbuf("junk", [P, width], BF16)
        stat = s.sbuf("stat", [P, 2, 4])
        v_stat = s.sbuf("v_stat", [P, 3, groups])
        y_stat = s.sbuf("y_stat", [P, 4])
        h_hi = s.sbuf("h_hi", [P, 2, rows, P], F32R)
        h_lo = s.sbuf("h_lo", [P, 2, rows, P], F32R)
        u_act = s.sbuf("u_act", [P, 2, BANK])
        v_act = s.sbuf("v_act", [P, BANK])
        v_sq = s.sbuf("v_sq", [P, BANK])
        v_norm = s.sbuf("v_norm", [P, BANK])
        gated = s.sbuf("gated", [P, BANK])
        y_out = s.sbuf("y_out", [P, 2, BANK])
        ht_ps = s.psum("ht_ps", [P, rows, P])
        z_ps = s.psum("z_ps", [P, 2, BANK])
        mix_ps = s.psum("mix_ps", [P, groups, P])

        w_loaded = [s.sem(f"w_loaded{i}") for i in range(2)]
        consts_loaded, spatial_loaded = s.sem("consts_loaded"), s.sem("spatial_loaded")
        masked, spatial_t, spatial_ready = s.sem("masked"), s.sem("spatial_t"), s.sem("spatial_ready")
        w_hi_done, w_lo_done = s.sem("w_hi_done"), s.sem("w_lo_done")
        x_loaded = [s.sem(f"x_loaded{i}") for i in range(2)]
        squared, meaned, rooted, h_done = s.sem("squared"), s.sem("meaned"), s.sem("rooted"), s.sem("h_done")
        ht_done, hh_done, hl_done = s.sem("ht_done"), s.sem("hh_done"), s.sem("hl_done")
        zu_done, zv_done, u_done, v_done = s.sem("zu_done"), s.sem("zv_done"), s.sem("u_done"), s.sem("v_done")
        v_squared, v_meaned, v_rooted, v_scaled, v_ready = (s.sem("v_squared"), s.sem("v_meaned"), s.sem("v_rooted"),
                                                            s.sem("v_scaled"), s.sem("v_ready"))
        mixed, gate_done, y_squared, y_meaned, y_rooted, y_done = (s.sem("mixed"), s.sem("gate_done"), s.sem("y_squared"),
                                                                   s.sem("y_meaned"), s.sem("y_rooted"), s.sem("y_done"))
        stored = [s.sem(f"stored{i}") for i in range(2)]

        def by_group(tile):
            return tile.rearrange("p (g c) -> p g c", g=groups)

        def per_group(col):
            return col.unsqueeze(2).broadcast_to([P, groups, chan])

        def rounds(engine, body):
            body(0, 0, True, False)
            body(0, 1, False, False)
            with engine.Fori(1, tiles // 2 - 1) as j:
                body(j, 0, False, False)
                body(j, 1, False, False)
            body(tiles // 2 - 1, 0, False, False)
            body(tiles // 2 - 1, 1, False, True)

        with nc.Block() as block:
            @block.sync
            def _(sp):
                sp.dma_start(gains[:], gain.partition_broadcast(P)).then_inc(consts_loaded, 16)
                sp.dma_start(v_gains[:], v_gain.rearrange("g c -> (g c)").partition_broadcast(P)).then_inc(consts_loaded, 16)
                sp.dma_start(out_gains[:], out_gain.partition_broadcast(P)).then_inc(consts_loaded, 16)
                with nc.allow_non_contiguous_dma(reason="512 biases, once"):
                    sp.dma_start(bias[:], b_spatial.rearrange("g t -> t g")).then_inc(consts_loaded, 16)

                def load_x(t, slot):
                    sp.dma_start(xs[:, slot], x[bass.ds(t * P, P), :]).then_inc(x_loaded[slot], 16)

                load_x(0, 0)
                load_x(1, 1)
                sp.dma_start(ws_raw[:], w_spatial.rearrange("g t s -> t g s")).then_inc(spatial_loaded, 16)
                for r in range(rows):
                    if r >= 2:
                        sp.wait_ge(w_lo_done, r - 1)
                    sp.dma_start(w_raw[:, r % 2], w_in[r * P:(r + 1) * P, 0:cols]).then_inc(w_loaded[r % 2], 16)

                def store(t, slot):
                    sp.wait_ge(y_done, t + 1)
                    sp.dma_start(ya[bass.ds(t * P, P), :], y_out[:, slot]).then_inc(stored[slot], 16)

                with sp.Fori(0, tiles // 2 - 1) as j:
                    for slot in range(2):
                        sp.wait_ge(h_done, 2 * j + slot + 1)
                        load_x(2 * j + slot + 2, slot)
                        store(2 * j + slot, slot)
                for slot in range(2):
                    store(tiles - 2 + slot, slot)
                for slot in range(2):
                    sp.wait_ge(stored[slot], 16 * tiles // 2)

            @block.gpsimd
            def _(pool):
                pool.wait_ge(spatial_loaded, 16)
                nc.gpsimd.affine_select(out=ws_raw[:], in_=ws_raw[:], compare_op=ALU.is_ge, fill=0.0, base=0,
                                        pattern=[[0, groups], [-1, P]], channel_multiplier=1).then_inc(masked, 1)

                def root(t, slot):
                    pool.wait_ge(meaned, t + 1)
                    nc.gpsimd.tensor_tensor(stat[:, slot, 2:3], stat[:, slot, 1:2], half[:, 0:1], ALU.pow).then_inc(rooted, 1)

                def root_y(t):
                    pool.wait_ge(y_meaned, t + 1)
                    nc.gpsimd.tensor_tensor(y_stat[:, 2:3], y_stat[:, 1:2], half[:, 0:1], ALU.pow).then_inc(y_rooted, 1)

                root(0, 0)

                def tile(j, slot, first, last):
                    t = 2 * j + slot
                    if not last:
                        root(t + 1, 1 - slot)
                    if not first:
                        root_y(t - 1)
                    pool.wait_ge(v_meaned, t + 1)
                    nc.gpsimd.tensor_tensor(v_stat[:, 2], v_stat[:, 1], half[:, 0:groups], ALU.pow).then_inc(v_rooted, 1)

                rounds(pool, tile)
                root_y(tiles - 1)

            @block.scalar
            def _(act):
                nc.scalar.preload_act_table(ACT.Gelu_apprx_tanh)

                def square(j, slot):
                    act.wait_ge(x_loaded[slot], 16 * (j + 1))
                    nc.scalar.activation(junk[:], xs[:, slot], ACT.Square, accum_out=stat[:, slot, 0:1]).then_inc(squared, 1)

                def high_h(t, slot):
                    act.wait_ge(ht_done, t + 1)
                    for part in range(2):
                        last = nc.scalar.copy(h_hi[:, slot, 4 * part:4 * part + 4], ht_ps[:, 4 * part:4 * part + 4])
                    last.then_inc(hh_done, 1)

                def square_y(t):
                    act.wait_ge(gate_done, t + 1)
                    nc.scalar.activation(junk[:, 0:BANK], gated[:], ACT.Square, accum_out=y_stat[:, 0:1]).then_inc(y_squared, 1)

                square(0, 0)
                for r in range(rows):
                    act.wait_ge(w_loaded[r % 2], 16 * (r // 2 + 1))
                    nc.scalar.copy(w_hi[:, r], w_raw[:, r % 2]).then_inc(w_hi_done, 1)
                high_h(0, 0)

                def tile(j, slot, first, last):
                    t = 2 * j + slot
                    if not last:
                        square(j + slot, 1 - slot)
                    act.wait_ge(zu_done, t + 1)
                    if not first:
                        act.wait_ge(gate_done, t - 1)
                    nc.scalar.activation(u_act[:, slot], z_ps[:, 0], ACT.Gelu_apprx_tanh).then_inc(u_done, 1)
                    if not first:
                        square_y(t - 1)
                    act.wait_ge(zv_done, t + 1)
                    act.wait_ge(v_scaled, t)
                    nc.scalar.activation(v_act[:], z_ps[:, 1], ACT.Gelu_apprx_tanh).then_inc(v_done, 1)
                    if not last:
                        high_h(t + 1, 1 - slot)

                rounds(act, tile)
                square_y(tiles - 1)

            @block.vector
            def _(dve):
                dve.wait_ge(consts_loaded, 64)

                def norm(t, slot):
                    dve.wait_ge(squared, t + 1)
                    nc.vector.tensor_scalar(stat[:, slot, 1:2], stat[:, slot, 0:1], 1.0 / width, EPS, ALU.mult, ALU.add).then_inc(meaned, 1)
                    dve.wait_ge(rooted, t + 1)
                    nc.vector.scalar_tensor_tensor(out=hs[:, slot], in0=xs[:, slot], scalar=stat[:, slot, 2:3], in1=gains[:],
                                                   op0=ALU.mult, op1=ALU.mult).then_inc(h_done, 1)

                def low_h(t, slot):
                    dve.wait_ge(hh_done, t + 1)
                    for part in range(2):
                        cut = slice(4 * part, 4 * part + 4)
                        last = nc.vector.tensor_tensor(h_lo[:, slot, cut], ht_ps[:, cut], as_f32(h_hi[:, slot, cut]), ALU.subtract)
                    last.then_inc(hl_done, 1)

                def gate(j, t, slot):
                    dve.wait_ge(mixed, t + 1)
                    dve.wait_ge(y_squared, t)
                    for g in range(groups):
                        last = nc.vector.scalar_tensor_tensor(
                            out=gated[:, g * P:(g + 1) * P], in0=mix_ps[:, g], scalar=bias[:, g:g + 1],
                            in1=u_act[:, slot, g * P:(g + 1) * P], op0=ALU.add, op1=ALU.mult)
                    last.then_inc(gate_done, 1)
                    dve.wait_ge(y_squared, t + 1)
                    nc.vector.tensor_scalar(y_stat[:, 1:2], y_stat[:, 0:1], 1.0 / BANK, EPS, ALU.mult, ALU.add).then_inc(y_meaned, 1)
                    dve.wait_ge(y_rooted, t + 1)
                    dve.wait_ge(stored[slot], 16 * j)
                    nc.vector.scalar_tensor_tensor(out=y_out[:, slot], in0=gated[:], scalar=y_stat[:, 2:3], in1=out_gains[:],
                                                   op0=ALU.mult, op1=ALU.mult).then_inc(y_done, 1)

                norm(0, 0)
                for r in range(rows):
                    dve.wait_ge(w_hi_done, r + 1)
                    nc.vector.tensor_tensor(w_lo[:, r], w_raw[:, r % 2], as_f32(w_hi[:, r]), ALU.subtract).then_inc(w_lo_done, 1)
                dve.wait_ge(spatial_t, 1)
                nc.vector.tensor_copy(ws_t[:], mix_ps[:]).then_inc(spatial_ready, 1)
                low_h(0, 0)

                def tile(j, slot, first, last):
                    t = 2 * j + slot
                    if not last:
                        norm(t + 1, 1 - slot)
                    if not first:
                        gate(j + slot - 1, t - 1, 1 - slot)
                    if not last:
                        low_h(t + 1, 1 - slot)
                    dve.wait_ge(v_done, t + 1)
                    nc.vector.tensor_tensor(v_sq[:], v_act[:], v_act[:], ALU.mult).then_inc(v_squared, 1)
                    dve.wait_ge(v_squared, 2 * t + 1)
                    nc.vector.tensor_reduce(v_stat[:, 0], by_group(v_sq[:]), AX.X, ALU.add).then_inc(v_squared, 1)
                    dve.wait_ge(v_squared, 2 * t + 2)
                    nc.vector.tensor_scalar(v_stat[:, 1], v_stat[:, 0], 1.0 / chan, EPS, ALU.mult, ALU.add).then_inc(v_meaned, 1)
                    dve.wait_ge(v_rooted, t + 1)
                    nc.vector.tensor_tensor(by_group(v_sq[:]), by_group(v_act[:]), per_group(v_stat[:, 2]), ALU.mult).then_inc(v_scaled, 1)
                    dve.wait_ge(v_scaled, t + 1)
                    dve.wait_ge(mixed, t)
                    nc.vector.tensor_tensor(v_norm[:], v_sq[:], v_gains[:], ALU.mult).then_inc(v_ready, 1)

                rounds(dve, tile)
                gate(tiles // 2 - 1, tiles - 1, 1)

            @block.tensor
            def _(pe):
                def transpose_h(t, slot):
                    pe.wait_ge(h_done, t + 1)
                    pe.wait_ge(hl_done, t)
                    for r in range(rows):
                        last = nc.tensor.transpose(ht_ps[:, r], hs[:, slot, r * P:(r + 1) * P], ident)
                    last.then_inc(ht_done, 1)

                def product(slot, chunk, done):
                    for r in range(rows):
                        last = split_product(nc.tensor, z_ps[:, chunk], h_hi[:, slot, r], h_lo[:, slot, r],
                                             w_hi[:, r, chunk * BANK:(chunk + 1) * BANK],
                                             w_lo[:, r, chunk * BANK:(chunk + 1) * BANK], r == 0, r == rows - 1)
                    last.then_inc(done, 1)

                def mix(t):
                    pe.wait_ge(v_ready, t + 1)
                    pe.wait_ge(gate_done, t)
                    for g in range(groups):
                        last = nc.tensor.matmul(mix_ps[:, g], ws_t[:, g], v_norm[:, g * P:(g + 1) * P], start=True, stop=True)
                    last.then_inc(mixed, 1)

                pe.wait_ge(masked, 1)
                for g in range(groups):
                    last = nc.tensor.transpose(mix_ps[:, g], ws_raw[:, g], ident)
                last.then_inc(spatial_t, 1)
                transpose_h(0, 0)
                pe.wait_ge(w_lo_done, rows)
                pe.wait_ge(spatial_ready, 1)

                def tile(j, slot, first, last):
                    t = 2 * j + slot
                    pe.wait_ge(hl_done, t + 1)
                    pe.wait_ge(u_done, t)
                    product(slot, 0, zu_done)
                    if not first:
                        mix(t - 1)
                    pe.wait_ge(v_done, t)
                    product(slot, 1, zv_done)
                    if not last:
                        transpose_h(t + 1, 1 - slot)

                rounds(pe, tile)
                mix(tiles - 1)


def attend_stick(nc, qt, kt, v, ident, ident_bf, above, yb, spare):
    heads, parts, tokens = qt.shape
    head_dim = parts // 2
    tiles = tokens // P
    per = BANK // P
    units = []
    for i in range(tiles):
        for c in range(i // per, -1, -1):
            keys = (i % per + 1) * P if c == i // per else BANK
            units.append((i, c, keys, c == i // per, c == 0))
    n_units = len(units)
    group_end = [max(u for u in range(n_units) if units[u][0] // per == g) + 1 for g in range(tiles // per)]
    by_dve = [u % 3 == 2 for u in range(n_units)]
    SLOTS = 4
    DVE_AT, WEIGHT_AT, T_AT, AV_AT, OUT_AT = 1, 2, 3, 4, 5

    with ExitStack() as stack:
        s = Scope(nc, stack, "stick")
        q_sb = s.sbuf("q", [P, tokens], F32R)
        k_hi = s.sbuf("k_hi", [P, 2 * tokens], F32R)
        k_lo = s.sbuf("k_lo", [P, 2 * tokens], F32R)
        v_sb = s.sbuf("v", [P, 2 * tiles * head_dim])
        soft = s.sbuf("soft", [P, SLOTS, BANK])
        sp_sb = s.sbuf("sp", [P, 2, BANK])
        rest = s.sbuf("rest", [P, 2, BANK])
        weight = s.sbuf("weight", [P, SLOTS, BANK])
        weight_t = s.sbuf("weight_t", [P, 2, per, P])
        z_ps = s.psum("z_ps", [P, SLOTS, BANK])
        t_ps = s.psum("t_ps", [P, 2, per, P])
        o_ps = s.psum("o_ps", [P, 2, BANK])

        zeros = s.sbuf("zeros", [P, spare.shape[1]])

        zeroed, spare_cleared = s.sem("zeroed"), s.sem("spare_cleared")
        kv_loaded = s.sem("kv_loaded")
        q_loaded = [s.sem(f"q_loaded{g}") for g in range(tiles // per)]
        z_done, exp_done, ln_done, sp_done, rest_done, exponent_done, weight_done = (
            s.sem(n) for n in ("z_done", "exp_done", "ln_done", "sp_done", "rest_done", "exponent_done", "weight_done"))
        t_done, copied_act, copied_dve, av_done, o_out = (
            s.sem(n) for n in ("t_done", "copied_act", "copied_dve", "av_done", "o_out"))

        def copies(u, dve):
            return sum(by_dve[x] == dve for x in range(u + 1))

        def wait_copy(engine, h, u):
            if u < 0:
                h, u = h - 1, u + n_units
            dve = by_dve[u]
            engine.wait_ge(copied_dve if dve else copied_act, h * copies(n_units - 1, dve) + copies(u, dve))

        def rounds(engine, lag, step):
            def head(h, first, over):
                for u in over:
                    def at(k, u=u):
                        back = u - k
                        if back >= n_units:
                            return None
                        if back >= 0:
                            return h, back
                        return None if first else (h - 1, back + n_units)
                    step(h, u, at)
            head(0, True, range(n_units))
            with engine.Fori(1, heads) as h:
                head(h, False, range(n_units))
            head(heads - 1, False, range(n_units, n_units + lag))

        with nc.Block() as block:
            @block.gpsimd
            def _(pool):
                nc.gpsimd.memset(zeros[:], 0.0).then_inc(zeroed, 1)
                pool.wait_ge(zeroed, 1)
                with pool.Fori(0, spare.shape[0] // P) as b:
                    pool.dma_start(spare[bass.ds(b * P, P), :], zeros[:]).then_inc(spare_cleared, 16)
                pool.wait_ge(spare_cleared, 16 * (spare.shape[0] // P))

            @block.sync
            def _(sp):
                def load_kv(h):
                    at = (h % 2) * tokens
                    for to, part in ((k_hi, 0), (k_lo, head_dim)):
                        for side in range(2):
                            sp.dma_start(as_f32(to[side * head_dim:(side + 1) * head_dim, bass.ds(at, tokens)]),
                                         kt[bass.ds(h, 1), part:part + head_dim, :].rearrange("o p t -> (o p) t")).then_inc(kv_loaded, 16)
                    sp.dma_start(v_sb[:, bass.ds((h % 2) * tiles * head_dim, tiles * head_dim)].rearrange("p (n d) -> p n d", n=tiles),
                                 v.rearrange("(n p) c -> p n c", p=P)[:, :, bass.ds(h * head_dim, head_dim)]).then_inc(kv_loaded, 16)

                def load_q(h, g):
                    cut = slice(g * BANK, (g + 1) * BANK)
                    sp.dma_start(as_f32(q_sb[:, cut]), qt[bass.ds(h, 1), :, cut].rearrange("o p t -> (o p) t")).then_inc(q_loaded[g], 16)

                load_q(0, 0)
                load_kv(0)
                for g in range(1, tiles // per):
                    load_q(0, g)
                with sp.Fori(0, heads - 1) as h:
                    sp.wait_ge(av_done, h * n_units)
                    sp.wait_ge(kv_loaded, 80 * (h + 1))
                    load_kv(h + 1)
                    for g in range(tiles // per):
                        sp.wait_ge(z_done, h * n_units + group_end[g])
                        load_q(h + 1, g)

            @block.tensor
            def _(pe):
                def step(h, u, at):
                    if at(0):
                        i, c, keys, head_of_tile, _ = units[u]
                        if u == 0:
                            pe.wait_ge(kv_loaded, 80 * (h + 1))
                        if u == 0 or group_end[i // per - 1] == u:
                            pe.wait_ge(q_loaded[i // per], 16 * (h + 1))
                        if at(SLOTS):
                            pe.wait_ge(exponent_done, h * n_units + u - SLOTS + 1)
                        out = z_ps[:, u % SLOTS, 0:keys]
                        base = (h % 2) * tokens + c * BANK
                        queries = q_sb[:, i * P:(i + 1) * P]
                        nc.tensor.matmul(out, queries, k_hi[:, bass.ds(base, keys)], start=True, stop=False)
                        last = nc.tensor.matmul(out, queries, k_lo[:, bass.ds(base, keys)], start=False, stop=not head_of_tile)
                        if head_of_tile:
                            last = nc.tensor.matmul(z_ps[:, u % SLOTS, keys - P:keys], ident_bf, above, start=False, stop=True)
                        last.then_inc(z_done, 1)
                    if at(T_AT):
                        g, w = at(T_AT)
                        pe.wait_ge(weight_done, g * n_units + w + 1)
                        if at(T_AT + 2):
                            wait_copy(pe, g, w - 2)
                        for b in range(units[w][2] // P):
                            last = nc.tensor.transpose(t_ps[:, w % 2, b], weight[:, w % SLOTS, b * P:(b + 1) * P], ident)
                        last.then_inc(t_done, 1)
                    if at(AV_AT):
                        g, w = at(AV_AT)
                        i, c, keys, head_of_tile, end_of_tile = units[w]
                        wait_copy(pe, g, w)
                        if head_of_tile and (i >= 2 or not (isinstance(g, int) and g == 0)):
                            pe.wait_ge(o_out, g * tiles + i - 1)
                        for b in range(keys // P):
                            last = nc.tensor.matmul(
                                o_ps[:, i % 2, 0:head_dim], weight_t[:, w % 2, b],
                                v_sb[:, bass.ds((g % 2) * tiles * head_dim + (c * per + b) * head_dim, head_dim)],
                                start=head_of_tile and b == 0, stop=end_of_tile and b == keys // P - 1)
                        last.then_inc(av_done, 1)

                rounds(pe, AV_AT, step)

            @block.scalar
            def _(act):
                nc.scalar.preload_act_table_set("natural_log_exp_and_others")

                def step(h, u, at):
                    if at(0):
                        keys = units[u][2]
                        act.wait_ge(z_done, h * n_units + u + 1)
                        if at(SLOTS):
                            act.wait_ge(sp_done, h * n_units + u - SLOTS + 1)
                        nc.scalar.activation(soft[:, u % SLOTS, 0:keys], z_ps[:, u % SLOTS, 0:keys], ACT.Exp).then_inc(exp_done, 1)
                    if at(0):
                        act.wait_ge(exp_done, h * n_units + u + 1)
                        nc.scalar.activation(soft[:, u % SLOTS, 0:units[u][2]], soft[:, u % SLOTS, 0:units[u][2]], ACT.Ln, bias=1.0).then_inc(ln_done, 1)
                    if at(WEIGHT_AT):
                        g, w = at(WEIGHT_AT)
                        keys = units[w][2]
                        act.wait_ge(exponent_done, g * n_units + w + 1)
                        nc.scalar.activation(weight[:, w % SLOTS, 0:keys], weight[:, w % SLOTS, 0:keys], ACT.Exp).then_inc(weight_done, 1)
                    if at(T_AT) and not by_dve[at(T_AT)[1]]:
                        g, w = at(T_AT)
                        act.wait_ge(t_done, g * n_units + w + 1)
                        if at(T_AT + 2):
                            act.wait_ge(av_done, g * n_units + w - 1)
                        blocks = units[w][2] // P
                        nc.scalar.copy(weight_t[:, w % 2, 0:blocks], t_ps[:, w % 2, 0:blocks]).then_inc(copied_act, 1)
                    if at(OUT_AT) and units[at(OUT_AT)[1]][4]:
                        g, w = at(OUT_AT)
                        i = units[w][0]
                        act.wait_ge(av_done, g * n_units + w + 1)
                        nc.scalar.copy(yb[:, i, bass.ds(g * head_dim, head_dim)], o_ps[:, i % 2, 0:head_dim]).then_inc(o_out, 1)

                rounds(act, OUT_AT, step)

            @block.vector
            def _(dve):
                def step(h, u, at):
                    if at(DVE_AT):
                        g, u = at(DVE_AT)
                        keys, head_of_tile = units[u][2:4]
                        n = g * n_units + u
                        dve.wait_ge(ln_done, n + 1)
                        nc.vector.scalar_tensor_tensor(out=sp_sb[:, u % 2, 0:keys], in0=soft[:, u % SLOTS, 0:keys], scalar=20.0,
                                                       in1=z_ps[:, u % SLOTS, 0:keys], op0=ALU.min, op1=ALU.max).then_inc(sp_done, 1)
                        dve.wait_ge(sp_done, n + 1)
                        start = 0.0 if head_of_tile else rest[:, (u - 1) % 2, 0:1]
                        back = sp_sb[:, u % 2, 0:keys][:, ::-1]
                        nc.vector.tensor_tensor_scan(rest[:, u % 2, 0:keys][:, ::-1], back, back, start,
                                                     ALU.add, ALU.bypass).then_inc(rest_done, 1)
                        dve.wait_ge(rest_done, n + 1)
                        if at(DVE_AT + SLOTS):
                            dve.wait_ge(t_done, n - SLOTS + 1)
                        nc.vector.tensor_tensor(weight[:, u % SLOTS, 0:keys], z_ps[:, u % SLOTS, 0:keys], rest[:, u % 2, 0:keys],
                                                ALU.subtract).then_inc(exponent_done, 1)
                    if at(T_AT) and by_dve[at(T_AT)[1]]:
                        g, w = at(T_AT)
                        dve.wait_ge(t_done, g * n_units + w + 1)
                        if at(T_AT + 2):
                            dve.wait_ge(av_done, g * n_units + w - 1)
                        blocks = units[w][2] // P
                        nc.vector.tensor_copy(weight_t[:, w % 2, 0:blocks], t_ps[:, w % 2, 0:blocks]).then_inc(copied_dve, 1)

                rounds(dve, T_AT, step)


def project_memory(nc, mem, gain, w_k, w_v, ident, half, key_t, value):
    slots, width = mem.shape
    tiles, rows = slots // P, width // P
    with ExitStack() as stack:
        s = Scope(nc, stack, "mem")
        wk = s.sbuf("wk", [P, rows, width])
        wv = s.sbuf("wv", [P, rows, width])
        gains = s.sbuf("gains", [P, width])
        ms = s.sbuf("ms", [P, tiles, width])
        junk = s.sbuf("junk", [P, tiles, width], BF16)
        stat = s.sbuf("stat", [P, tiles, 4])
        m_t = s.sbuf("m_t", [P, rows, slots])
        t_ps = s.psum("t_ps", [P, rows, P])
        z_ps = s.psum("z_ps", [P, 4, BANK])
        loaded, wk_loaded, wv_loaded = s.sem("loaded"), s.sem("wk_loaded"), s.sem("wv_loaded")
        squared, meaned, rooted, normed, t_done, t_out = (s.sem(n) for n in ("squared", "meaned", "rooted", "normed", "t_done", "t_out"))
        z_done, z_act, z_dve = s.sem("z_done"), s.sem("z_act"), s.sem("z_dve")
        products = [("k", n) for n in range(rows // 2)] + [("v", n) for n in range(2 * tiles)]

        def target(kind, n):
            if kind == "k":
                return key_t[:, 2 * n:2 * n + 2].rearrange("p r m -> p (r m)")
            return value[:, n // 2, (n % 2) * BANK:(n % 2 + 1) * BANK]

        with nc.Block() as block:
            @block.sync
            def _(sp):
                sp.dma_start(ms[:], mem.rearrange("(n p) d -> p n d", p=P)).then_inc(loaded, 16)
                sp.dma_start(gains[:], gain.partition_broadcast(P)).then_inc(loaded, 16)
                sp.dma_start(wk[:], w_k.rearrange("(r p) c -> p r c", p=P)).then_inc(wk_loaded, 16)
                sp.dma_start(wv[:], w_v.rearrange("(r p) c -> p r c", p=P)).then_inc(wv_loaded, 16)

            @block.gpsimd
            def _(pool):
                pool.wait_ge(meaned, 1)
                nc.gpsimd.tensor_tensor(stat[:, :, 2], stat[:, :, 1], half[:, 0:tiles], ALU.pow).then_inc(rooted, 1)

            @block.scalar
            def _(act):
                act.wait_ge(loaded, 32)
                for n in range(tiles):
                    last = nc.scalar.activation(junk[:, n], ms[:, n], ACT.Square, accum_out=stat[:, n, 0:1])
                last.then_inc(squared, 1)
                for n, (kind, at) in enumerate(products):
                    if n % 2 == 0:
                        act.wait_ge(z_done, n + 1)
                        nc.scalar.copy(target(kind, at), z_ps[:, n % 4]).then_inc(z_act, 1)

            @block.vector
            def _(dve):
                dve.wait_ge(squared, 1)
                nc.vector.tensor_scalar(stat[:, :, 1], stat[:, :, 0], 1.0 / width, EPS, ALU.mult, ALU.add).then_inc(meaned, 1)
                dve.wait_ge(rooted, 1)
                for n in range(tiles):
                    nc.vector.scalar_tensor_tensor(out=ms[:, n], in0=ms[:, n], scalar=stat[:, n, 2:3], in1=gains[:],
                                                   op0=ALU.mult, op1=ALU.mult).then_inc(normed, 1)
                for n in range(tiles):
                    dve.wait_ge(t_done, n + 1)
                    nc.vector.tensor_copy(m_t[:, :, n * P:(n + 1) * P], t_ps[:]).then_inc(t_out, 1)
                for n, (kind, at) in enumerate(products):
                    if n % 2 == 1:
                        dve.wait_ge(z_done, n + 1)
                        nc.vector.tensor_copy(target(kind, at), z_ps[:, n % 4]).then_inc(z_dve, 1)

            @block.tensor
            def _(pe):
                for n in range(tiles):
                    pe.wait_ge(normed, n + 1)
                    pe.wait_ge(t_out, n)
                    for r in range(rows):
                        last = nc.tensor.transpose(t_ps[:, r], ms[:, n, r * P:(r + 1) * P], ident)
                    last.then_inc(t_done, 1)
                pe.wait_ge(t_out, tiles)
                pe.wait_ge(wk_loaded, 16)
                for n, (kind, at) in enumerate(products):
                    if (kind, at) == ("v", 0):
                        pe.wait_ge(wv_loaded, 16)
                    if n >= 4:
                        pe.wait_ge(z_act if n % 2 == 0 else z_dve, n // 2 - 1)
                    if kind == "k":
                        for half_bank in range(2):
                            for r in range(rows):
                                last = nc.tensor.matmul(z_ps[:, n % 4, half_bank * slots:(half_bank + 1) * slots],
                                                        wk[:, r, (2 * at + half_bank) * P:(2 * at + half_bank + 1) * P],
                                                        m_t[:, r], start=r == 0, stop=r == rows - 1)
                    else:
                        for r in range(rows):
                            last = nc.tensor.matmul(z_ps[:, n % 4], m_t[:, r, (at // 2) * P:(at // 2 + 1) * P],
                                                    wv[:, r, (at % 2) * BANK:(at % 2 + 1) * BANK], start=r == 0, stop=r == rows - 1)
                    last.then_inc(z_done, 1)


def project_out(nc, ya, yb, gain_b, w_out, x, ident, half, x1):
    tokens, width = x.shape
    tiles, rows = tokens // P, width // P
    with ExitStack() as stack:
        s = Scope(nc, stack, "out")
        w_hi = s.sbuf("w_hi", [P, rows, width], F32R)
        w_lo = s.sbuf("w_lo", [P, rows, width], F32R)
        w_raw = s.sbuf("w_raw", [P, 2, width])
        gains = s.sbuf("gains", [P, BANK])
        ys = s.sbuf("ys", [P, 2, width])
        xs = s.sbuf("xs", [P, 2, width])
        junk = s.sbuf("junk", [P, BANK], BF16)
        stat = s.sbuf("stat", [P, 2, 4])
        y_hi = s.sbuf("y_hi", [P, 2, rows, P], F32R)
        y_lo = s.sbuf("y_lo", [P, 2, rows, P], F32R)
        t_ps = s.psum("t_ps", [P, rows, P])
        z_ps = s.psum("z_ps", [P, 2, 2, BANK])

        w_loaded = [s.sem(f"w_loaded{i}") for i in range(2)]
        gains_loaded, w_hi_done, w_lo_done = s.sem("gains_loaded"), s.sem("w_hi_done"), s.sem("w_lo_done")
        y_loaded = [s.sem(f"y_loaded{i}") for i in range(2)]
        x_loaded = [s.sem(f"x_loaded{i}") for i in range(2)]
        stored = [s.sem(f"stored{i}") for i in range(2)]
        squared, meaned, rooted, normed = s.sem("squared"), s.sem("meaned"), s.sem("rooted"), s.sem("normed")
        t_done, hi_done, lo_done, z_done, added = (s.sem(n) for n in ("t_done", "hi_done", "lo_done", "z_done", "added"))

        def rounds(engine, body):
            with engine.Fori(0, tiles // 2 - 1) as j:
                body(j, 0, False)
                body(j, 1, False)
            body(tiles // 2 - 1, 0, False)
            body(tiles // 2 - 1, 1, True)

        with nc.Block() as block:
            @block.sync
            def _(sp):
                sp.dma_start(gains[:], gain_b.partition_broadcast(P)).then_inc(gains_loaded, 16)

                def load_y(t, slot):
                    sp.dma_start(ys[:, slot, 0:BANK], ya[bass.ds(t * P, P), :]).then_inc(y_loaded[slot], 16)

                def load_x(t, slot):
                    sp.dma_start(xs[:, slot], x[bass.ds(t * P, P), :]).then_inc(x_loaded[slot], 16)

                load_y(0, 0)
                load_y(1, 1)
                for r in range(rows):
                    if r >= 2:
                        sp.wait_ge(w_lo_done, r - 1)
                    sp.dma_start(w_raw[:, r % 2], w_out[r * P:(r + 1) * P, :]).then_inc(w_loaded[r % 2], 16)
                load_x(0, 0)
                load_x(1, 1)

                def tile(j, slot, last):
                    t = 2 * j + slot
                    sp.wait_ge(t_done, t + 1)
                    if not isinstance(j, int):
                        load_y(t + 2, slot)
                    sp.wait_ge(added, t + 1)
                    sp.dma_start(x1[bass.ds(t * P, P), :], xs[:, slot]).then_inc(stored[slot], 16)
                    if not isinstance(j, int):
                        sp.wait_ge(stored[slot], 16 * (j + 1))
                        load_x(t + 2, slot)

                rounds(sp, tile)
                for slot in range(2):
                    sp.wait_ge(stored[slot], 16 * tiles // 2)

            @block.gpsimd
            def _(pool):
                def root(t, slot):
                    pool.wait_ge(meaned, t + 1)
                    nc.gpsimd.tensor_tensor(stat[:, slot, 2:3], stat[:, slot, 1:2], half[:, 0:1], ALU.pow).then_inc(rooted, 1)

                root(0, 0)

                def tile(j, slot, last):
                    if not last:
                        root(2 * j + slot + 1, 1 - slot)

                rounds(pool, tile)

            @block.scalar
            def _(act):
                def square(t, slot):
                    nc.scalar.activation(junk[:], yb[:, bass.ds(t, 1), :].rearrange("p o c -> p (o c)"), ACT.Square,
                                         accum_out=stat[:, slot, 0:1]).then_inc(squared, 1)

                def high(t, slot):
                    act.wait_ge(t_done, t + 1)
                    for part in range(2):
                        last = nc.scalar.copy(y_hi[:, slot, 4 * part:4 * part + 4], t_ps[:, 4 * part:4 * part + 4])
                    last.then_inc(hi_done, 1)

                square(0, 0)
                for r in range(rows):
                    act.wait_ge(w_loaded[r % 2], 16 * (r // 2 + 1))
                    nc.scalar.copy(w_hi[:, r], w_raw[:, r % 2]).then_inc(w_hi_done, 1)
                high(0, 0)

                def tile(j, slot, last):
                    if not last:
                        t = 2 * j + slot + 1
                        act.wait_ge(normed, t)
                        square(t, 1 - slot)
                        high(t, 1 - slot)

                rounds(act, tile)

            @block.vector
            def _(dve):
                dve.wait_ge(gains_loaded, 16)

                def norm(t, slot, wait_slot):
                    dve.wait_ge(squared, t + 1)
                    nc.vector.tensor_scalar(stat[:, slot, 1:2], stat[:, slot, 0:1], 1.0 / BANK, EPS, ALU.mult, ALU.add).then_inc(meaned, 1)
                    dve.wait_ge(rooted, t + 1)
                    if wait_slot:
                        dve.wait_ge(t_done, t - 1)
                    nc.vector.scalar_tensor_tensor(out=ys[:, slot, BANK:], in0=yb[:, bass.ds(t, 1), :].rearrange("p o c -> p (o c)"),
                                                   scalar=stat[:, slot, 2:3], in1=gains[:], op0=ALU.mult, op1=ALU.mult).then_inc(normed, 1)

                def low(t, slot):
                    dve.wait_ge(hi_done, t + 1)
                    for part in range(2):
                        cut = slice(4 * part, 4 * part + 4)
                        last = nc.vector.tensor_tensor(y_lo[:, slot, cut], t_ps[:, cut], as_f32(y_hi[:, slot, cut]), ALU.subtract)
                    last.then_inc(lo_done, 1)

                norm(0, 0, False)
                for r in range(rows):
                    dve.wait_ge(w_hi_done, r + 1)
                    nc.vector.tensor_tensor(w_lo[:, r], w_raw[:, r % 2], as_f32(w_hi[:, r]), ALU.subtract).then_inc(w_lo_done, 1)
                low(0, 0)

                def tile(j, slot, last):
                    t = 2 * j + slot
                    if not last:
                        norm(t + 1, 1 - slot, True)
                        low(t + 1, 1 - slot)
                    dve.wait_ge(x_loaded[slot], 16 * (j + 1))
                    for chunk in range(2):
                        dve.wait_ge(z_done, 2 * t + chunk + 1)
                        cut = slice(chunk * BANK, (chunk + 1) * BANK)
                        last_add = nc.vector.tensor_tensor(xs[:, slot, cut], z_ps[:, slot, chunk], xs[:, slot, cut], ALU.add)
                    last_add.then_inc(added, 1)

                rounds(dve, tile)

            @block.tensor
            def _(pe):
                def transpose_y(j, t, slot):
                    pe.wait_ge(normed, t + 1)
                    pe.wait_ge(y_loaded[slot], 16 * (j + 1))
                    pe.wait_ge(lo_done, t)
                    for r in range(rows):
                        last = nc.tensor.transpose(t_ps[:, r], ys[:, slot, r * P:(r + 1) * P], ident)
                    last.then_inc(t_done, 1)

                transpose_y(0, 0, 0)
                pe.wait_ge(w_lo_done, rows)

                def tile(j, slot, last):
                    t = 2 * j + slot
                    pe.wait_ge(lo_done, t + 1)
                    if slot == 0:
                        pe.wait_ge(added, 2 * j)
                    for chunk in range(2):
                        for r in range(rows):
                            last_mm = split_product(nc.tensor, z_ps[:, slot, chunk], y_hi[:, slot, r], y_lo[:, slot, r],
                                                    w_hi[:, r, chunk * BANK:(chunk + 1) * BANK],
                                                    w_lo[:, r, chunk * BANK:(chunk + 1) * BANK], r == 0, r == rows - 1)
                        last_mm.then_inc(z_done, 1)
                        if chunk == 0 and not last:
                            transpose_y(j + slot, t + 1, 1 - slot)

                rounds(pe, tile)


def attend_memory(nc, x1, gain_q, w_q, w_o, key_t, value, gain_moe, w_group, w_router, b_group, b_router,
                  ident, half, x2, hm, logits):
    tokens, width = x1.shape
    tiles, rows = tokens // P, width // P
    slots = key_t.shape[2]
    heads = width // slots
    per_head = rows // heads
    keys = slots // P
    n_group, n_logit = w_group.shape[1], logits.shape[2]
    scale = (width // heads) ** -0.5
    with ExitStack() as stack:
        s = Scope(nc, stack, "cross")
        wq_hi = s.sbuf("wq_hi", [P, rows, width], F32R)
        wq_lo = s.sbuf("wq_lo", [P, rows, width], F32R)
        wo_hi = s.sbuf("wo_hi", [P, rows, width], F32R)
        wo_lo = s.sbuf("wo_lo", [P, rows, width], F32R)
        w_logit = s.sbuf("w_logit", [P, rows, n_logit])
        b_logit = s.sbuf("b_logit", [P, n_logit])
        q_gains = s.sbuf("q_gains", [P, rows])
        m_gains = s.sbuf("m_gains", [P, width])
        xs = s.sbuf("xs", [P, 2, width])
        h_hi = s.sbuf("h_hi", [P, rows, P], F32R)
        h_lo = s.sbuf("h_lo", [P, rows, P], F32R)
        q_and_p = s.sbuf("q_and_p", [P, 2, width])
        q_t = s.sbuf("q_t", [P, rows, P])
        p_t = s.sbuf("p_t", [P, heads * keys, P])
        o_hi = s.sbuf("o_hi", [P, rows, P], F32R)
        o_lo = s.sbuf("o_lo", [P, rows, P], F32R)
        x2_sb = s.sbuf("x2", [P, width])
        hm_sb = s.sbuf("hm", [P, width])
        hm_t = s.sbuf("hm_t", [P, rows, P])
        junk = s.sbuf("junk", [P, width], BF16)
        stat = s.sbuf("stat", [P, 4])
        m_stat = s.sbuf("m_stat", [P, 4])
        soft_stat = s.sbuf("soft_stat", [P, 4, heads])
        h_ps = s.psum("h_ps", [P, rows, P])
        s_ps = s.psum("s_ps", [P, rows, P])
        z_ps = s.psum("z_ps", [P, rows, P])
        x_ps = s.psum("x_ps", [P, rows, P])
        q_sb, p_sb = q_and_p[:, 0], q_and_p[:, 1]

        w_loaded = [s.sem(f"w_loaded{i}") for i in range(2)]
        consts_loaded, gains_loaded = s.sem("consts_loaded"), s.sem("gains_loaded")
        x_loaded = [s.sem(f"x_loaded{i}") for i in range(2)]
        names = ("w_hi_done w_lo_done res_loaded x2_stored hm_stored squared meaned rooted h_done "
                 "ht_done hh_done hl_done zq_done q_act q_dve tq_done qt_act qt_dve scored maxed negated exped summed inverted "
                 "p_done tp_done pt_act pt_dve ot_done oh_done ol_done xo_done added m_squared m_meaned m_rooted "
                 "hm_done tm_done mt_out logit_done logit_out")
        (w_hi_done, w_lo_done, res_loaded, x2_stored, hm_stored, squared, meaned, rooted, h_done,
         ht_done, hh_done, hl_done, zq_done, q_act, q_dve, tq_done, qt_act, qt_dve, scored, maxed, negated, exped, summed, inverted,
         p_done, tp_done, pt_act, pt_dve, ot_done, oh_done, ol_done, xo_done, added, m_squared, m_meaned, m_rooted,
         hm_done, tm_done, mt_out, logit_done, logit_out) = (s.sem(n) for n in names.split())

        def rounds(engine, step):
            step(-1, 1, True, False, False, True)
            step(0, 0, True, True, False, True)
            with engine.Fori(0, tiles // 2 - 2) as j:
                step(2 * j + 1, 1, True, True, True, True)
                step(2 * j + 2, 0, True, True, True, True)
            step(tiles - 3, 1, True, True, True, True)
            step(tiles - 2, 0, True, True, True, False)
            step(tiles - 1, 1, False, True, True, False)
            step(tiles, 0, False, False, True, False)

        with nc.Block() as block:
            @block.sync
            def _(sp):
                def load_x(t, slot):
                    sp.dma_start(xs[:, slot], x1[bass.ds(t * P, P), :]).then_inc(x_loaded[slot], 16)

                def load_residual(t):
                    sp.dma_start(x2_sb[:], x1[bass.ds(t * P, P), :]).then_inc(res_loaded, 16)

                with nc.allow_non_contiguous_dma(reason="1024 gains, once"):
                    sp.dma_start(q_gains[:], gain_q.rearrange("(r p) -> p r", p=P)).then_inc(gains_loaded, 16)
                load_x(0, 0)
                load_x(1, 1)
                load_residual(0)
                for n in range(2 * rows):
                    w, r = (w_q, n) if n < rows else (w_o, n - rows)
                    if n >= 2:
                        sp.wait_ge(w_lo_done, n - 1)
                    sp.dma_start(q_and_p[:, n % 2], w[r * P:(r + 1) * P, :]).then_inc(w_loaded[n % 2], 16)
                sp.dma_start(m_gains[:], gain_moe.partition_broadcast(P)).then_inc(consts_loaded, 16)
                sp.dma_start(b_logit[:, 0:n_group], b_group.partition_broadcast(P)).then_inc(consts_loaded, 16)
                sp.dma_start(b_logit[:, n_group:], b_router.partition_broadcast(P)).then_inc(consts_loaded, 16)
                sp.dma_start(w_logit[:, :, 0:n_group], w_group.rearrange("(r p) c -> p r c", p=P)).then_inc(consts_loaded, 16)
                sp.dma_start(w_logit[:, :, n_group:], w_router.rearrange("(r p) c -> p r c", p=P)).then_inc(consts_loaded, 16)

                def step(b, slot, a_on, b_on, c_on, f_on):
                    if f_on and b_on:
                        sp.wait_ge(ht_done, b + 1)
                        load_x(b + 2, slot)
                    if b_on:
                        sp.wait_ge(added, b + 1)
                        sp.dma_start(x2[bass.ds(b * P, P), :], x2_sb[:]).then_inc(x2_stored, 16)
                        sp.wait_ge(hm_done, b + 1)
                        sp.dma_start(hm[bass.ds(b * P, P), :], hm_sb[:]).then_inc(hm_stored, 16)
                    if b_on and a_on:
                        sp.wait_ge(x2_stored, 16 * (b + 1))
                        load_residual(b + 1)

                rounds(sp, step)
                sp.wait_ge(x2_stored, 16 * tiles)
                sp.wait_ge(hm_stored, 16 * tiles)

            @block.gpsimd
            def _(pool):
                def root(t):
                    pool.wait_ge(meaned, t + 1)
                    nc.gpsimd.tensor_tensor(stat[:, 2:3], stat[:, 1:2], half[:, 0:1], ALU.pow).then_inc(rooted, 1)

                root(0)

                def step(b, slot, a_on, b_on, c_on, f_on):
                    if f_on:
                        root(b + 2)
                    if b_on:
                        pool.wait_ge(m_meaned, b + 1)
                        nc.gpsimd.tensor_tensor(m_stat[:, 2:3], m_stat[:, 1:2], half[:, 0:1], ALU.pow).then_inc(m_rooted, 1)

                rounds(pool, step)

            @block.scalar
            def _(act):
                nc.scalar.preload_act_table(ACT.Exp)

                def square(t, slot, nth):
                    act.wait_ge(x_loaded[slot], 16 * nth)
                    nc.scalar.activation(junk[:], xs[:, slot], ACT.Square, accum_out=stat[:, 0:1]).then_inc(squared, 1)

                square(0, 0, 1)
                act.wait_ge(gains_loaded, 16)
                for n in range(2 * rows):
                    act.wait_ge(w_loaded[n % 2], 16 * (n // 2 + 1))
                    if n < rows:
                        nc.scalar.activation(wq_hi[:, n], q_and_p[:, n % 2], ACT.Copy, scale=q_gains[:, n:n + 1]).then_inc(w_hi_done, 1)
                    else:
                        nc.scalar.copy(wo_hi[:, n - rows], q_and_p[:, n % 2]).then_inc(w_hi_done, 1)

                def step(b, slot, a_on, b_on, c_on, f_on):
                    a, c, f = b + 1, b - 1, b + 2
                    if a_on:
                        act.wait_ge(ht_done, a + 1)
                        for part in range(2):
                            last = nc.scalar.copy(h_hi[:, 4 * part:4 * part + 4], h_ps[:, 4 * part:4 * part + 4])
                        last.then_inc(hh_done, 1)
                        act.wait_ge(zq_done, a + 1)
                        nc.scalar.copy(q_sb[:, 0:BANK], z_ps[:, 0:4].rearrange("p r t -> p (r t)")).then_inc(q_act, 1)
                    if b_on:
                        act.wait_ge(tp_done, b + 1)
                        nc.scalar.copy(p_t[:, 0:4], s_ps[:, 0:4]).then_inc(pt_act, 1)
                    if c_on:
                        act.wait_ge(tm_done, c + 1)
                        for part in range(2):
                            last = nc.scalar.copy(hm_t[:, 4 * part:4 * part + 4], x_ps[:, 4 * part:4 * part + 4])
                        last.then_inc(mt_out, 1)
                    if a_on:
                        act.wait_ge(tq_done, a + 1)
                        nc.scalar.copy(q_t[:, 0:4], h_ps[:, 0:4]).then_inc(qt_act, 1)
                    if b_on:
                        act.wait_ge(ot_done, b + 1)
                        for part in range(2):
                            last = nc.scalar.copy(o_hi[:, 4 * part:4 * part + 4], z_ps[:, 4 * part:4 * part + 4])
                        last.then_inc(oh_done, 1)
                    if a_on:
                        act.wait_ge(negated, a + 1)
                        for h in range(heads):
                            last = nc.scalar.activation(p_sb[:, h * slots:(h + 1) * slots],
                                                        s_ps[:, keys * h:keys * (h + 1)].rearrange("p r t -> p (r t)"), ACT.Exp,
                                                        bias=soft_stat[:, 1, h:h + 1], scale=scale, accum_out=soft_stat[:, 2, h:h + 1])
                        last.then_inc(exped, 1)
                    if f_on:
                        act.wait_ge(h_done, f)
                        square(f, slot, f // 2 + 1)
                    if b_on:
                        act.wait_ge(added, b + 1)
                        if f_on:
                            act.wait_ge(squared, f + 1)
                        act.wait_ge(hm_done, b)
                        nc.scalar.activation(junk[:], x2_sb[:], ACT.Square, accum_out=m_stat[:, 0:1]).then_inc(m_squared, 1)

                rounds(act, step)

            @block.vector
            def _(dve):
                def norm(t, slot):
                    dve.wait_ge(squared, t + 1)
                    nc.vector.tensor_scalar(stat[:, 1:2], stat[:, 0:1], 1.0 / width, EPS, ALU.mult, ALU.add).then_inc(meaned, 1)
                    dve.wait_ge(rooted, t + 1)
                    nc.vector.tensor_scalar(xs[:, slot], xs[:, slot], stat[:, 2:3], None, ALU.mult).then_inc(h_done, 1)

                norm(0, 0)
                dve.wait_ge(gains_loaded, 16)
                for n in range(2 * rows):
                    dve.wait_ge(w_hi_done, n + 1)
                    if n < rows:
                        nc.vector.scalar_tensor_tensor(out=wq_lo[:, n], in0=q_and_p[:, n % 2], scalar=q_gains[:, n:n + 1],
                                                       in1=as_f32(wq_hi[:, n]), op0=ALU.mult, op1=ALU.subtract).then_inc(w_lo_done, 1)
                    else:
                        nc.vector.tensor_tensor(wo_lo[:, n - rows], q_and_p[:, n % 2], as_f32(wo_hi[:, n - rows]),
                                                ALU.subtract).then_inc(w_lo_done, 1)
                dve.wait_ge(consts_loaded, 80)

                def step(b, slot, a_on, b_on, c_on, f_on):
                    a, c, f = b + 1, b - 1, b + 2
                    if a_on:
                        dve.wait_ge(hh_done, a + 1)
                        for part in range(2):
                            cut = slice(4 * part, 4 * part + 4)
                            last = nc.vector.tensor_tensor(h_lo[:, cut], h_ps[:, cut], as_f32(h_hi[:, cut]), ALU.subtract)
                        last.then_inc(hl_done, 1)
                        dve.wait_ge(zq_done, a + 1)
                        nc.vector.tensor_copy(q_sb[:, BANK:], z_ps[:, 4:].rearrange("p r t -> p (r t)")).then_inc(q_dve, 1)
                    if b_on:
                        dve.wait_ge(tp_done, b + 1)
                        nc.vector.tensor_copy(p_t[:, 4:], s_ps[:, 4:]).then_inc(pt_dve, 1)
                    if a_on:
                        dve.wait_ge(tq_done, a + 1)
                        nc.vector.tensor_copy(q_t[:, 4:], h_ps[:, 4:]).then_inc(qt_dve, 1)
                    if b_on:
                        dve.wait_ge(oh_done, b + 1)
                        for part in range(2):
                            cut = slice(4 * part, 4 * part + 4)
                            last = nc.vector.tensor_tensor(o_lo[:, cut], z_ps[:, cut], as_f32(o_hi[:, cut]), ALU.subtract)
                        last.then_inc(ol_done, 1)
                    if c_on:
                        dve.wait_ge(logit_done, c + 1)
                        nc.vector.tensor_tensor(logits[:, bass.ds(c, 1), :], x_ps[:, 0:1, 0:n_logit],
                                                b_logit[:].rearrange("p (o c) -> p o c", o=1), ALU.add).then_inc(logit_out, 1)
                    if a_on:
                        dve.wait_ge(scored, a + 1)
                        nc.vector.tensor_reduce(soft_stat[:, 0], s_ps[:].rearrange("p (h k) t -> p h (k t)", h=heads), AX.X, ALU.max).then_inc(maxed, 1)
                        dve.wait_ge(maxed, a + 1)
                        nc.vector.tensor_scalar(soft_stat[:, 1], soft_stat[:, 0], -scale, None, ALU.mult).then_inc(negated, 1)
                        dve.wait_ge(exped, a + 1)
                        nc.vector.reciprocal(soft_stat[:, 3], soft_stat[:, 2]).then_inc(inverted, 1)
                        dve.wait_ge(inverted, a + 1)
                        weights = p_sb.rearrange("p (h m) -> p h m", h=heads)
                        nc.vector.tensor_tensor(weights, weights, soft_stat[:, 3].unsqueeze(2).broadcast_to([P, heads, slots]),
                                                ALU.mult).then_inc(p_done, 1)
                    if f_on:
                        norm(f, slot)
                    if b_on:
                        dve.wait_ge(res_loaded, 16 * (b + 1))
                        for chunk in range(2):
                            dve.wait_ge(xo_done, 2 * b + chunk + 1)
                            cut = slice(chunk * BANK, (chunk + 1) * BANK)
                            last = nc.vector.tensor_tensor(x2_sb[:, cut], x_ps[:, 4 * chunk:4 * chunk + 4].rearrange("p r t -> p (r t)"),
                                                           x2_sb[:, cut], ALU.add)
                        last.then_inc(added, 1)
                        dve.wait_ge(m_squared, b + 1)
                        nc.vector.tensor_scalar(m_stat[:, 1:2], m_stat[:, 0:1], 1.0 / width, EPS, ALU.mult, ALU.add).then_inc(m_meaned, 1)
                        dve.wait_ge(m_rooted, b + 1)
                        dve.wait_ge(tm_done, b)
                        dve.wait_ge(hm_stored, 16 * b)
                        nc.vector.scalar_tensor_tensor(out=hm_sb[:], in0=x2_sb[:], scalar=m_stat[:, 2:3], in1=m_gains[:],
                                                       op0=ALU.mult, op1=ALU.mult).then_inc(hm_done, 1)

                rounds(dve, step)

            @block.tensor
            def _(pe):
                def transposes(out, of, done):
                    for r in range(rows):
                        last = nc.tensor.transpose(out[:, r], of[:, r * P:(r + 1) * P], ident)
                    last.then_inc(done, 1)

                def step(b, slot, a_on, b_on, c_on, f_on):
                    a, c = b + 1, b - 1
                    if a_on:
                        pe.wait_ge(h_done, a + 1)
                        pe.wait_ge(qt_act, a)
                        pe.wait_ge(qt_dve, a)
                        transposes(h_ps, xs[:, 1 - slot], ht_done)
                        if not b_on:
                            pe.wait_ge(w_lo_done, rows)
                        pe.wait_ge(hl_done, a + 1)
                        pe.wait_ge(ol_done, a - 1 if b_on else 0)
                        for chunk in range(2):
                            cut = slice(chunk * BANK, (chunk + 1) * BANK)
                            out = z_ps[:, 4 * chunk:4 * chunk + 4].rearrange("p r t -> p (r t)")
                            for r in range(rows):
                                last = split_product(nc.tensor, out, h_hi[:, r], h_lo[:, r], wq_hi[:, r, cut], wq_lo[:, r, cut],
                                                     r == 0, r == rows - 1)
                        last.then_inc(zq_done, 1)
                    if b_on:
                        pe.wait_ge(p_done, b + 1)
                        transposes(s_ps, p_sb, tp_done)
                    if c_on:
                        pe.wait_ge(hm_done, c + 1)
                        transposes(x_ps, hm_sb[:], tm_done)
                    if a_on:
                        pe.wait_ge(q_act, a + 1)
                        pe.wait_ge(q_dve, a + 1)
                        transposes(h_ps, q_sb, tq_done)
                    if b_on:
                        pe.wait_ge(pt_act, b + 1)
                        pe.wait_ge(pt_dve, b + 1)
                        for r in range(rows):
                            for k in range(keys):
                                last = nc.tensor.matmul(z_ps[:, r], value[:, k, r * P:(r + 1) * P], p_t[:, (r // per_head) * keys + k],
                                                        start=k == 0, stop=k == keys - 1)
                        last.then_inc(ot_done, 1)
                    if c_on:
                        pe.wait_ge(mt_out, c + 1)
                        for r in range(rows):
                            last = nc.tensor.matmul(x_ps[:, 0, 0:n_logit], hm_t[:, r], w_logit[:, r], start=r == 0, stop=r == rows - 1)
                        last.then_inc(logit_done, 1)
                    if a_on:
                        pe.wait_ge(qt_act, a + 1)
                        pe.wait_ge(qt_dve, a + 1)
                        for h in range(heads):
                            for r in range(per_head):
                                last = nc.tensor.matmul(s_ps[:, keys * h:keys * (h + 1)].rearrange("p r t -> p (r t)"),
                                                        q_t[:, per_head * h + r], key_t[:, per_head * h + r],
                                                        start=r == 0, stop=r == per_head - 1)
                        last.then_inc(scored, 1)
                    if b_on:
                        if not c_on:
                            pe.wait_ge(w_lo_done, 2 * rows)
                            pe.wait_ge(consts_loaded, 80)
                        pe.wait_ge(ol_done, b + 1)
                        if c_on:
                            pe.wait_ge(logit_out, b)
                        for chunk in range(2):
                            cut = slice(chunk * BANK, (chunk + 1) * BANK)
                            out = x_ps[:, 4 * chunk:4 * chunk + 4].rearrange("p r t -> p (r t)")
                            for r in range(rows):
                                last = split_product(nc.tensor, out, o_hi[:, r], o_lo[:, r], wo_hi[:, r, cut], wo_lo[:, r, cut],
                                                     r == 0, r == rows - 1)
                            last.then_inc(xo_done, 1)

                rounds(pe, step)


def route(nc, logits, n_group, gates, dests, slot_tokens, block_end, block_expert, block_kind):
    tiles, n_logit = logits.shape[1], logits.shape[2]
    experts = n_logit - n_group
    members = experts // n_group
    blocks = slot_tokens.shape[1]
    LOW, LOWER = -1e30, -3e30
    MARK = -1024.0
    with ExitStack() as stack:
        s = Scope(nc, stack, "route")
        wide = [P, tiles, experts]
        index = s.sbuf("index", [P, tiles, experts])
        g_max = s.sbuf("g_max", [P, tiles])
        g_work = s.sbuf("g_work", [P, tiles, n_group])
        g_pick = s.sbuf("g_pick", [P, tiles, n_group])
        g_least = s.sbuf("g_least", [P, tiles])
        g_shift = s.sbuf("g_shift", [P, tiles, n_group])
        g_sum = s.sbuf("g_sum", [P, tiles])
        g_gate = s.sbuf("g_gate", [P, tiles])
        shut = s.sbuf("shut", [P, tiles, n_group])
        e_in = s.sbuf("e_in", wide)
        e_top = s.sbuf("e_top", [P, 2, tiles])
        e_work = s.sbuf("e_work", wide)
        e_least = s.sbuf("e_least", [P, tiles])
        pick = s.sbuf("pick", [P, 2, tiles, experts])
        both = s.sbuf("both", wide, BF16)
        ratio = s.sbuf("ratio", [P, tiles])
        share = s.sbuf("share", [P, 2, tiles])
        before = s.sbuf("before", [P, P], BF16)
        ones = s.sbuf("ones", [P, P], BF16)
        counts = s.sbuf("counts", [P, tiles + 1, experts])
        need = s.sbuf("need", [P, experts])
        need_int = s.sbuf("need_int", [P, experts], I32)
        ends = s.sbuf("ends", [P, experts])
        starts = s.sbuf("starts", [P, experts])
        place = s.sbuf("place", wide)
        dest = s.sbuf("dest", [P, 2, tiles])
        dest_int = s.sbuf("dest_int", [P, 2, tiles], I32)
        dest_row = s.sbuf("dest_row", [P, 2, tiles], I32)
        dest_part = s.sbuf("dest_part", [P, 2, 2, tiles])
        lanes = s.sbuf("lanes", [P, P])
        token = s.sbuf("token", [P, tiles])
        in_slot = s.sbuf("in_slot", [P, 2, P])
        in_block = s.sbuf("in_block", [P, 2, blocks])
        block_no = s.sbuf("block_no", [P, blocks, experts])
        passed = s.sbuf("passed", [P, blocks, experts])
        expert_f = s.sbuf("expert_f", [P, blocks])
        fresh = s.sbuf("fresh", [P, blocks])
        rank_ps = s.psum("rank_ps", [P, tiles, experts])
        total_ps = s.psum("total_ps", [P, tiles, experts])
        slot_ps = s.psum("slot_ps", [P, blocks])
        built, stepped, exped, ranked = s.sem("built"), s.sem("stepped"), s.sem("exped"), s.sem("ranked")
        cut, slotted = s.sem("cut"), s.sem("slotted")
        pairs = 2 * tiles
        marks = {}

        def along(col):
            return col.unsqueeze(2).broadcast_to([P, tiles, experts])

        with nc.Block() as block:
            @block.gpsimd
            def _(pool):
                nc.gpsimd.iota(index[:], [[0, tiles], [1, experts]], base=0, channel_multiplier=0,
                               allow_small_or_imprecise_dtypes=True).then_inc(built, 1)
                nc.gpsimd.iota(lanes[:], [[1, P]], base=0, channel_multiplier=0, allow_small_or_imprecise_dtypes=True).then_inc(built, 1)
                nc.gpsimd.iota(token[:], [[P, tiles]], base=0, channel_multiplier=1, allow_small_or_imprecise_dtypes=True).then_inc(built, 1)
                nc.gpsimd.iota(block_no[:], [[1, blocks], [0, experts]], base=0, channel_multiplier=0,
                               allow_small_or_imprecise_dtypes=True).then_inc(built, 1)
                nc.gpsimd.memset(ones[:], 1.0).then_inc(built, 1)
                pool.wait_ge(built, 5)
                nc.gpsimd.affine_select(out=before[:], in_=ones[:], compare_op=ALU.is_gt, fill=0.0, base=0,
                                        pattern=[[1, P]], channel_multiplier=-1).then_inc(built, 1)

            @block.vector
            def _(dve):
                count = [0]

                def link(ins, mark=None):
                    count[0] += 1
                    ins.then_inc(stepped, 1)
                    dve.wait_ge(stepped, count[0])
                    if mark:
                        marks[mark] = count[0]

                dve.wait_ge(built, 6)
                g_in = logits[:, :, 0:n_group]
                g_index = index[:, :, 0:n_group]
                per_g = [P, tiles, n_group]
                link(nc.vector.tensor_reduce(g_max[:], g_in, AX.X, ALU.max))
                link(nc.vector.tensor_tensor(g_shift[:], g_in, g_max[:].unsqueeze(2).broadcast_to(per_g), ALU.subtract), "g_shift")
                link(nc.vector.tensor_tensor(g_work[:], g_in, g_max[:].unsqueeze(2).broadcast_to(per_g), ALU.is_equal))
                link(nc.vector.scalar_tensor_tensor(out=g_work[:], in0=g_work[:], scalar=MARK, in1=g_index, op0=ALU.mult, op1=ALU.add))
                link(nc.vector.tensor_reduce(g_least[:], g_work[:], AX.X, ALU.min))
                link(nc.vector.tensor_tensor(g_pick[:], g_work[:], g_least[:].unsqueeze(2).broadcast_to(per_g), ALU.is_equal))
                link(nc.vector.tensor_scalar(shut[:], g_pick[:], -LOW, LOW, ALU.mult, ALU.add))
                for g in range(n_group):
                    span = slice(g * members, (g + 1) * members)
                    wide_g = [P, tiles, members]
                    link(nc.vector.tensor_tensor(e_in[:, :, span], logits[:, :, n_group + g * members:n_group + (g + 1) * members],
                                                 g_pick[:, :, g:g + 1].broadcast_to(wide_g), ALU.mult))
                    link(nc.vector.tensor_tensor(e_in[:, :, span], e_in[:, :, span], shut[:, :, g:g + 1].broadcast_to(wide_g), ALU.add))
                for k in range(2):
                    link(nc.vector.tensor_reduce(e_top[:, k], e_in[:], AX.X, ALU.max))
                    link(nc.vector.tensor_tensor(e_work[:], e_in[:], along(e_top[:, k]), ALU.is_equal))
                    link(nc.vector.scalar_tensor_tensor(out=e_work[:], in0=e_work[:], scalar=MARK, in1=index[:], op0=ALU.mult, op1=ALU.add))
                    link(nc.vector.tensor_reduce(e_least[:], e_work[:], AX.X, ALU.min))
                    link(nc.vector.tensor_tensor(pick[:, k], e_work[:], along(e_least[:]), ALU.is_equal))
                    if k == 0:
                        link(nc.vector.scalar_tensor_tensor(out=e_in[:], in0=pick[:, 0], scalar=LOWER, in1=e_in[:], op0=ALU.mult, op1=ALU.add))
                link(nc.vector.tensor_tensor(both[:], pick[:, 0], pick[:, 1], ALU.add), "both")
                link(nc.vector.tensor_tensor(ratio[:], e_top[:, 1], e_top[:, 0], ALU.subtract), "ratio")
                dve.wait_ge(exped, 2)
                link(nc.vector.tensor_reduce(g_sum[:], g_shift[:], AX.X, ALU.add))
                link(nc.vector.reciprocal(g_gate[:], g_sum[:]))
                link(nc.vector.tensor_scalar(share[:, 1], ratio[:], 1.0, None, ALU.add))
                link(nc.vector.reciprocal(share[:, 0], share[:, 1]))
                link(nc.vector.tensor_tensor(gates[:, 0], share[:, 0], g_gate[:], ALU.mult))
                link(nc.vector.tensor_tensor(gates[:, 1], gates[:, 0], ratio[:], ALU.mult))
                dve.wait_ge(ranked, 2)
                link(nc.vector.memset(counts[:, 0], 0.0))
                for t in range(tiles):
                    link(nc.vector.tensor_tensor(counts[:, t + 1], counts[:, t], total_ps[:, t], ALU.add))
                link(nc.vector.tensor_scalar(need_int[:], counts[:, tiles], float(P - 1), None, ALU.add))
                link(nc.vector.tensor_scalar(need_int[:], need_int[:], P.bit_length() - 1, None, ALU.arith_shift_right))
                link(nc.vector.tensor_scalar(need[:], need_int[:], 1.0, None, ALU.max))
                link(nc.vector.tensor_tensor_scan(ends[:], need[:], need[:], 0.0, ALU.add, ALU.bypass))
                link(nc.vector.tensor_copy(block_end[:], ends[:]))
                link(nc.vector.tensor_tensor(starts[:], ends[:], need[:], ALU.subtract))
                link(nc.vector.tensor_scalar(starts[:], starts[:], float(P), None, ALU.mult))
                link(nc.vector.tensor_tensor(place[:], rank_ps[:], counts[:, 0:tiles], ALU.add))
                link(nc.vector.tensor_tensor(place[:], place[:], starts[:].unsqueeze(1).broadcast_to(wide), ALU.add))
                for k in range(2):
                    link(nc.vector.tensor_tensor(e_work[:], place[:], pick[:, k], ALU.mult))
                    link(nc.vector.tensor_reduce(dest[:, k], e_work[:], AX.X, ALU.add))
                link(nc.vector.tensor_copy(dest_int[:], dest[:]))
                link(nc.vector.tensor_copy(dests[:], dest[:]))
                link(nc.vector.tensor_scalar(dest_row[:], dest_int[:], P.bit_length() - 1, None, ALU.arith_shift_right))
                link(nc.vector.tensor_copy(dest_part[:, 0], dest_row[:]))
                link(nc.vector.tensor_scalar(dest_row[:], dest_int[:], P - 1, None, ALU.bitwise_and))
                link(nc.vector.tensor_copy(dest_part[:, 1], dest_row[:]))
                link(nc.vector.tensor_tensor(passed[:], ends[:].unsqueeze(1).broadcast_to([P, blocks, experts]), block_no[:], ALU.is_le))
                link(nc.vector.tensor_reduce(expert_f[:], passed[:], AX.X, ALU.add))
                link(nc.vector.tensor_scalar(expert_f[:], expert_f[:], float(experts - 1), None, ALU.min))
                link(nc.vector.tensor_copy(block_expert[:], expert_f[:]))
                link(nc.vector.tensor_tensor(fresh[:, 1:], expert_f[:, 1:], expert_f[:, 0:blocks - 1], ALU.not_equal))
                link(nc.vector.memset(fresh[:, 0:1], 1.0))
                link(nc.vector.tensor_scalar(expert_f[:], expert_f[:], float(experts - 1), 1.0, ALU.is_equal, ALU.add))
                link(nc.vector.tensor_tensor(fresh[:], fresh[:], expert_f[:], ALU.mult))
                link(nc.vector.tensor_copy(block_kind[:], fresh[:]))
                for n in range(pairs):
                    k, t = n % 2, n // 2
                    if n >= 2:
                        dve.wait_ge(slotted, n - 1)
                    nc.vector.tensor_scalar(in_slot[:, n % 2], lanes[:], dest_part[:, 1, k, t:t + 1], None, ALU.is_equal).then_inc(cut, 1)
                    nc.vector.tensor_scalar(in_block[:, n % 2], block_no[:, :, 0], dest_part[:, 0, k, t:t + 1], token[:, t:t + 1],
                                            ALU.is_equal, ALU.mult).then_inc(cut, 1)
                dve.wait_ge(slotted, pairs)
                link(nc.vector.tensor_copy(slot_tokens[:], slot_ps[:]))

            @block.scalar
            def _(act):
                act.wait_ge(stepped, marks["g_shift"])
                nc.scalar.activation(g_shift[:], g_shift[:], ACT.Exp).then_inc(exped, 1)
                act.wait_ge(stepped, marks["ratio"])
                nc.scalar.activation(ratio[:], ratio[:], ACT.Exp).then_inc(exped, 1)

            @block.tensor
            def _(pe):
                pe.wait_ge(built, 6)
                pe.wait_ge(stepped, marks["both"])
                choices = both[:].rearrange("p t e -> p (t e)")
                nc.tensor.matmul(rank_ps[:].rearrange("p t e -> p (t e)"), before[:], choices, start=True, stop=True).then_inc(ranked, 1)
                nc.tensor.matmul(total_ps[:].rearrange("p t e -> p (t e)"), ones[:], choices, start=True, stop=True).then_inc(ranked, 1)
                for n in range(pairs):
                    pe.wait_ge(cut, 2 * n + 2)
                    nc.tensor.matmul(slot_ps[:], in_slot[:, n % 2], in_block[:, n % 2], start=n == 0, stop=n == pairs - 1).then_inc(slotted, 1)


def run_experts(nc, hm, w1, w3, w2, slot_tokens, block_end, block_expert, block_kind, n_blocks, ident, ybuf):
    experts, width, hidden = w1.shape
    rows, h_rows = width // P, hidden // P
    set_size = 2 * rows * hidden
    chunk = 2 * BANK
    RING = 4
    with ExitStack() as stack:
        s = Scope(nc, stack, "moe")
        w13_hi, w13_lo = s.sbuf("w13_hi", [P, 2 * set_size], F32R), s.sbuf("w13_lo", [P, 2 * set_size], F32R)
        w2_hi, w2_lo = s.sbuf("w2_hi", [P, h_rows, width], F32R), s.sbuf("w2_lo", [P, h_rows, width], F32R)
        raw = s.sbuf("raw", [P, RING, chunk])
        now = s.sbuf("now", [P, 1], I32)
        xg = s.sbuf("xg", [P, width])
        x_hi, x_lo = s.sbuf("x_hi", [P, rows, P], F32R), s.sbuf("x_lo", [P, rows, P], F32R)
        g_sb = s.sbuf("g", [P, hidden])
        h_sb = s.sbuf("h", [P, hidden])
        h_hi, h_lo = s.sbuf("h_hi", [P, h_rows, P], F32R), s.sbuf("h_lo", [P, h_rows, P], F32R)
        y_sb = s.sbuf("y", [P, width])
        x_ps = s.psum("x_ps", [P, rows, P])
        g_ps = s.psum("g_ps", [P, hidden])
        u_ps = s.psum("u_ps", [P, hidden])
        h_ps = s.psum("h_ps", [P, h_rows, P])
        y_ps = s.psum("y_ps", [P, width])
        w13_loaded = [s.sem(f"w13_loaded{i}") for i in range(RING)]
        w2_loaded = [s.sem(f"w2_loaded{i}") for i in range(RING)]
        (w13_cut, w13_ready, w2_cut, w2_ready, listed, list_seen, gathered, xt_done, xh_done, xl_done, g_done, up_done, silu_done,
         gated, ht_done, hh_done, hl_done, y_done, y_free, stored, all_stored) = (
            s.sem(n) for n in ("w13_cut w13_ready w2_cut w2_ready listed list_seen gathered xt_done xh_done xl_done g_done up_done "
                               "silu_done gated ht_done hh_done hl_done y_done y_free stored all_stored").split())

        def blocks_in_use(engine):
            return engine.value_load(block_end[0:1, experts - 1:experts], min_val=experts, max_val=n_blocks)

        def rounds(engine, step):
            used = blocks_in_use(engine)
            step(0, True, True)
            with engine.Fori(1, used) as b:
                step(b, False, True)
            step(used, False, False)

        def cutting_rounds(engine, step):
            used = blocks_in_use(engine)
            step(0, True, True, 0, True, True)
            with engine.Fori(1, used) as b:
                kind = engine.value_load(block_kind[0:1, bass.ds(b, 1)], min_val=0, max_val=2)
                with engine.If(kind == 0):
                    step(b, False, True, None, False, False)
                with engine.Else():
                    with engine.If(kind == 1):
                        e = engine.value_load(block_expert[0:1, bass.ds(b, 1)], min_val=0, max_val=experts - 1)
                        step(b, False, True, e, True, True)
                    with engine.Else():
                        step(b, False, True, experts - 1, False, True)
                    engine.nop()
            step(used, False, False, None, False, False)

        def w13_at(e, i):
            return bass.ds((e % 2) * set_size + i * chunk, chunk)

        with nc.Block() as block:
            @block.sync
            def _(sp):
                def load_w13(e, i):
                    for half_of, w in enumerate((w1, w3)):
                        sp.dma_start(raw[:, i % RING, half_of * hidden:(half_of + 1) * hidden],
                                     w[bass.ds(e, 1), i * P:(i + 1) * P, :].rearrange("o p c -> (o p) c")).then_inc(w13_loaded[i % RING], 16)

                def load_w2(e, i):
                    sp.dma_start(raw[:, i % RING], w2[bass.ds(e, 1), i * P:(i + 1) * P, :].rearrange("o p c -> (o p) c")
                                 ).then_inc(w2_loaded[i % RING], 16)

                def load(e, first, last):
                    if not last:
                        for i in range(rows):
                            if i >= RING or first:
                                sp.wait_ge(w13_ready, rows * (e + 1) + i + 1 - RING)
                            else:
                                sp.wait_ge(w2_ready, h_rows * (e - 1) + i + 1)
                            load_w13(e + 1, i)
                    for i in range(h_rows):
                        if last:
                            sp.wait_ge(w2_ready, h_rows * (e - 1) + i + 1)
                        else:
                            sp.wait_ge(w13_ready, rows * (e + 2) + i + 1 - RING)
                        load_w2(e, i)

                for i in range(rows):
                    if i >= RING:
                        sp.wait_ge(w13_ready, i + 1 - RING)
                    load_w13(0, i)
                load(0, True, False)
                with sp.Fori(1, experts - 1) as e:
                    load(e, False, False)
                load(experts - 1, False, True)

            @block.gpsimd
            def _(pool):
                def gather(b):
                    if not isinstance(b, int):
                        pool.wait_ge(gathered, 16 * b)
                    nc.gpsimd.tensor_copy(now[:], slot_tokens[:, bass.ds(b, 1)]).then_inc(listed, 1)
                    if not isinstance(b, int):
                        pool.wait_ge(xt_done, b)
                    pool.wait_ge(listed, b + 1)
                    pool.sem_inc(list_seen, 1)
                    nc.gpsimd.indirect_dma_start(out=xg[:], out_offset=None, in_=hm,
                                                 in_offset=bass.IndirectOffsetOnAxis(ap=now[:].bitcast(U32), axis=0)).then_inc(gathered, 16)

                used = blocks_in_use(pool)
                gather(0)
                with pool.Fori(1, used + 1) as b:
                    gather(b)

            @block.scalar
            def _(act):
                nc.scalar.preload_act_table(ACT.Silu)
                act.sem_inc(y_free, 1)
                act.sem_inc(stored, 16)

                def cut_w13(e, these):
                    for i in these:
                        act.wait_ge(w13_loaded[i % RING], 32 * (2 * e + i // RING + 1))
                        nc.scalar.copy(w13_hi[:, w13_at(e, i)], raw[:, i % RING]).then_inc(w13_cut, 1)

                def high_x(b):
                    act.wait_ge(xt_done, b + 1)
                    if not isinstance(b, int) or b:
                        act.wait_ge(up_done, b)
                    for part in range(2):
                        cut = slice(part * rows // 2, (part + 1) * rows // 2)
                        last = nc.scalar.copy(x_hi[:, cut], x_ps[:, cut])
                    last.then_inc(xh_done, 1)

                cut_w13(0, range(rows))
                high_x(0)

                def step(b, first, more, e, with_w13, with_w2):
                    if with_w13:
                        if not first:
                            act.wait_ge(up_done, b)
                        cut_w13(e + 1, range(0, 4))
                    if more:
                        act.wait_ge(g_done, b + 1)
                        if not first:
                            act.wait_ge(gated, b)
                        nc.scalar.activation(g_sb[:], g_ps[:], ACT.Silu).then_inc(silu_done, 1)
                    if with_w13:
                        cut_w13(e + 1, range(4, 6))
                    if more:
                        high_x(b + 1)
                    if with_w13:
                        cut_w13(e + 1, range(6, rows))
                    if not first:
                        act.wait_ge(y_done, b)
                        act.wait_ge(stored, 16 * b)
                        for part in range(2):
                            last = nc.scalar.copy(y_sb[:, part * BANK:(part + 1) * BANK], y_ps[:, part * BANK:(part + 1) * BANK])
                        last.then_inc(y_free, 1)
                        act.wait_ge(y_free, b + 1)
                        act.dma_start(ybuf[bass.ds((b - 1) * P, P), :], y_sb[:]).then_inc(stored, 16)
                    if more:
                        act.wait_ge(ht_done, b + 1)
                        nc.scalar.copy(h_hi[:], h_ps[:]).then_inc(hh_done, 1)
                    if with_w2:
                        for i in range(h_rows):
                            act.wait_ge(w2_loaded[i % RING], 16 * (e + 1))
                            nc.scalar.copy(w2_hi[:, i], raw[:, i % RING]).then_inc(w2_cut, 1)

                cutting_rounds(act, step)
                act.wait_ge(stored, 16 * (blocks_in_use(act) + 1))
                act.sem_inc(all_stored, 1)

            @block.vector
            def _(dve):
                def cut_w13(e, these):
                    for i in these:
                        dve.wait_ge(w13_cut, rows * e + i + 1)
                        nc.vector.tensor_tensor(w13_lo[:, w13_at(e, i)], raw[:, i % RING], as_f32(w13_hi[:, w13_at(e, i)]),
                                                ALU.subtract).then_inc(w13_ready, 1)

                def low_x(b):
                    dve.wait_ge(xh_done, b + 1)
                    for part in range(2):
                        cut = slice(part * rows // 2, (part + 1) * rows // 2)
                        last = nc.vector.tensor_tensor(x_lo[:, cut], x_ps[:, cut], as_f32(x_hi[:, cut]), ALU.subtract)
                    last.then_inc(xl_done, 1)

                cut_w13(0, range(rows))
                low_x(0)

                def step(b, first, more, e, with_w13, with_w2):
                    if with_w13:
                        cut_w13(e + 1, range(0, 6))
                    if more:
                        dve.wait_ge(silu_done, b + 1)
                        dve.wait_ge(up_done, b + 1)
                        if not first:
                            dve.wait_ge(ht_done, b)
                        nc.vector.tensor_tensor(h_sb[:], u_ps[:], g_sb[:], ALU.mult).then_inc(gated, 1)
                        low_x(b + 1)
                    if with_w13:
                        cut_w13(e + 1, range(6, rows))
                    if more:
                        dve.wait_ge(hh_done, b + 1)
                        nc.vector.tensor_tensor(h_lo[:], h_ps[:], as_f32(h_hi[:]), ALU.subtract).then_inc(hl_done, 1)
                    if with_w2:
                        for i in range(h_rows):
                            dve.wait_ge(w2_cut, h_rows * e + i + 1)
                            nc.vector.tensor_tensor(w2_lo[:, i], raw[:, i % RING], as_f32(w2_hi[:, i]), ALU.subtract).then_inc(w2_ready, 1)

                cutting_rounds(dve, step)

            @block.tensor
            def _(pe):
                def transpose_x(b):
                    pe.wait_ge(gathered, 16 * (b + 1))
                    if not isinstance(b, int) or b:
                        pe.wait_ge(xl_done, b)
                    for r in range(rows):
                        last = nc.tensor.transpose(x_ps[:, r], xg[:, r * P:(r + 1) * P], ident)
                    last.then_inc(xt_done, 1)

                def expert_of(b):
                    return pe.value_load(block_expert[0:1, bass.ds(b, 1)], min_val=0, max_val=experts - 1)

                transpose_x(0)

                def step(b, first, more):
                    if more:
                        x = expert_of(b)
                        base = (x % 2) * set_size
                        pe.wait_ge(w13_ready, rows * (x + 1))
                        pe.wait_ge(xl_done, b + 1)
                        if not first:
                            pe.wait_ge(silu_done, b)
                        for out, at, done in ((g_ps, 0, g_done), (u_ps, hidden, up_done)):
                            if out is u_ps and not first:
                                pe.wait_ge(gated, b)
                            for r in range(rows):
                                cols = bass.ds(base + r * chunk + at, hidden)
                                last = split_product(nc.tensor, out[:], x_hi[:, r], x_lo[:, r], w13_hi[:, cols], w13_lo[:, cols],
                                                     r == 0, r == rows - 1)
                            last.then_inc(done, 1)
                        transpose_x(b + 1)
                    if not first:
                        pe.wait_ge(w2_ready, h_rows * (expert_of(b - 1) + 1))
                        pe.wait_ge(hl_done, b)
                        pe.wait_ge(y_free, b)
                        for part in range(2):
                            cols = slice(part * BANK, (part + 1) * BANK)
                            for r in range(h_rows):
                                last = split_product(nc.tensor, y_ps[:, cols], h_hi[:, r], h_lo[:, r], w2_hi[:, r, cols], w2_lo[:, r, cols],
                                                     r == 0, r == h_rows - 1)
                        last.then_inc(y_done, 1)
                    if more:
                        pe.wait_ge(gated, b + 1)
                        for r in range(h_rows):
                            last = nc.tensor.transpose(h_ps[:, r], h_sb[:, r * P:(r + 1) * P], ident)
                        last.then_inc(ht_done, 1)

                rounds(pe, step)


def combine(nc, x2, ybuf, gates, dests, gain, half, out):
    tokens, width = x2.shape
    tiles = tokens // P
    with ExitStack() as stack:
        s = Scope(nc, stack, "end")
        gains = s.sbuf("gains", [P, width])
        now = s.sbuf("now", [P, 2, 2], I32)
        xs = s.sbuf("xs", [P, 2, width])
        y0 = s.sbuf("y0", [P, 2, width])
        y1 = s.sbuf("y1", [P, 2, width])
        outs = s.sbuf("outs", [P, 2, width])
        junk = s.sbuf("junk", [P, width], BF16)
        stat = s.sbuf("stat", [P, 2, 4])
        gains_loaded, list_seen = s.sem("gains_loaded"), s.sem("list_seen")
        x_loaded, y0_loaded, y1_loaded, stored = ([s.sem(f"{n}{i}") for i in range(2)] for n in ("x_loaded", "y0_loaded", "y1_loaded", "stored"))
        listed, first_added, added, squared, meaned, rooted, done = (
            s.sem(n) for n in ("listed", "first_added", "added", "squared", "meaned", "rooted", "done"))

        def rounds(engine, tile):
            tile(0, 0, True)
            tile(0, 1, True)
            with engine.Fori(1, tiles // 2) as j:
                tile(j, 0, False)
                tile(j, 1, False)

        with nc.Block() as block:
            @block.sync
            def _(sp):
                sp.dma_start(gains[:], gain.partition_broadcast(P)).then_inc(gains_loaded, 16)

                def load(t, slot):
                    sp.dma_start(xs[:, slot], x2[bass.ds(t * P, P), :]).then_inc(x_loaded[slot], 16)

                load(0, 0)
                load(1, 1)

                def store(t, slot):
                    sp.wait_ge(done, t + 1)
                    sp.dma_start(out[bass.ds(t * P, P), :], outs[:, slot]).then_inc(stored[slot], 16)

                with sp.Fori(0, tiles // 2 - 1) as j:
                    for slot in range(2):
                        store(2 * j + slot, slot)
                        load(2 * j + slot + 2, slot)
                for slot in range(2):
                    store(tiles - 2 + slot, slot)
                for slot in range(2):
                    sp.wait_ge(stored[slot], 16 * tiles // 2)

            @block.gpsimd
            def _(pool):
                def gather(j, slot):
                    t = 2 * j + slot
                    pool.wait_ge(y0_loaded[slot], 16 * j)
                    pool.wait_ge(y1_loaded[slot], 16 * j)
                    for k in range(2):
                        nc.gpsimd.tensor_copy(now[:, slot, k:k + 1], dests[:, k, bass.ds(t, 1)]).then_inc(listed, 1)
                    pool.wait_ge(listed, 2 * t + 2)
                    pool.sem_inc(list_seen, 1)
                    for k, (y, loaded) in enumerate(((y0, y0_loaded), (y1, y1_loaded))):
                        nc.gpsimd.indirect_dma_start(out=y[:, slot], out_offset=None, in_=ybuf,
                                                     in_offset=bass.IndirectOffsetOnAxis(ap=now[:, slot, k:k + 1].bitcast(U32), axis=0)
                                                     ).then_inc(loaded[slot], 16)

                def root(t, slot):
                    pool.wait_ge(meaned, t + 1)
                    nc.gpsimd.tensor_tensor(stat[:, slot, 2:3], stat[:, slot, 1:2], half[:, 0:1], ALU.pow).then_inc(rooted, 1)

                gather(0, 0)
                gather(0, 1)
                with pool.Fori(0, tiles // 2 - 1) as j:
                    for slot in range(2):
                        root(2 * j + slot, slot)
                        pool.wait_ge(added, 2 * j + slot + 1)
                        gather(j + 1, slot)
                root(tiles - 2, 0)
                root(tiles - 1, 1)

            @block.scalar
            def _(act):
                def tile(j, slot, first):
                    t = 2 * j + slot
                    act.wait_ge(added, t + 1)
                    act.wait_ge(meaned, t)
                    if not first:
                        act.wait_ge(done, t - 1)
                    nc.scalar.activation(junk[:], xs[:, slot], ACT.Square, accum_out=stat[:, slot, 0:1]).then_inc(squared, 1)

                rounds(act, tile)

            @block.vector
            def _(dve):
                dve.wait_ge(gains_loaded, 16)

                def add(j, slot):
                    t = 2 * j + slot
                    dve.wait_ge(x_loaded[slot], 16 * (j + 1))
                    dve.wait_ge(y0_loaded[slot], 16 * (j + 1))
                    nc.vector.scalar_tensor_tensor(out=xs[:, slot], in0=y0[:, slot], scalar=gates[:, 0, bass.ds(t, 1)], in1=xs[:, slot],
                                                   op0=ALU.mult, op1=ALU.add).then_inc(first_added, 1)
                    dve.wait_ge(y1_loaded[slot], 16 * (j + 1))
                    dve.wait_ge(first_added, t + 1)
                    nc.vector.scalar_tensor_tensor(out=xs[:, slot], in0=y1[:, slot], scalar=gates[:, 1, bass.ds(t, 1)], in1=xs[:, slot],
                                                   op0=ALU.mult, op1=ALU.add).then_inc(added, 1)

                def finish(j, slot):
                    t = 2 * j + slot
                    dve.wait_ge(squared, t + 1)
                    nc.vector.tensor_scalar(stat[:, slot, 1:2], stat[:, slot, 0:1], 1.0 / width, EPS, ALU.mult, ALU.add).then_inc(meaned, 1)
                    dve.wait_ge(rooted, t + 1)
                    dve.wait_ge(stored[slot], 16 * j)
                    nc.vector.scalar_tensor_tensor(out=outs[:, slot], in0=xs[:, slot], scalar=stat[:, slot, 2:3], in1=gains[:],
                                                   op0=ALU.mult, op1=ALU.mult).then_inc(done, 1)

                add(0, 0)
                with dve.Fori(0, tiles // 2 - 1) as j:
                    add(j, 1)
                    finish(j, 0)
                    add(j + 1, 0)
                    finish(j, 1)
                add(tiles // 2 - 1, 1)
                finish(tiles // 2 - 1, 0)
                finish(tiles // 2 - 1, 1)


def set_constants(nc, ident, half, ident_bf, above):
    with ExitStack() as stack:
        s = Scope(nc, stack, "const")
        filled, masked = s.sem("filled"), s.sem("masked")
        with nc.Block() as block:
            @block.gpsimd
            def _(pool):
                nc.gpsimd.memset(ident[:], 0.0).then_inc(filled, 1)
                nc.gpsimd.memset(ident_bf[:], 0.0).then_inc(filled, 1)
                nc.gpsimd.memset(above[:], 0.0).then_inc(filled, 1)
                nc.gpsimd.memset(half[:], -0.5).then_inc(filled, 1)
                pool.wait_ge(filled, 4)
                for tile, compare, fill in ((ident, ALU.not_equal, 1.0), (ident_bf, ALU.not_equal, 1.0), (above, ALU.is_gt, -1e30)):
                    nc.gpsimd.affine_select(out=tile[:], in_=tile[:], compare_op=compare, fill=fill, base=0,
                                            pattern=[[-1, P]], channel_multiplier=1).then_inc(masked, 1)
                pool.wait_ge(masked, 3)


def build_trunk(nc, x, mem, norm_mix, w_in, v_norm, w_spatial, b_spatial, out_norm_a, out_norm_b, w_out, norm_cross, norm_mem,
                w_xq, w_xk, w_xv, w_xo, norm_moe, w_group, b_group, w_router, b_router, w1, w3, w2, norm_final, out):
    tokens, width = x.shape[1], x.shape[2]
    tiles, rows, slots = tokens // P, width // P, mem.shape[1]
    half_width, head_dim = width // 2, 64
    heads = half_width // head_dim
    n_group, experts, top_k = w_group.shape[2], w1.shape[1], 2
    n_blocks = (tokens * top_k - experts) // P + experts
    qt = nc.dram_tensor("qt_scratch", [heads, 2 * head_dim, tokens], F32).ap()
    kt = nc.dram_tensor("kt_scratch", [heads, 2 * head_dim, tokens], F32).ap()
    v = nc.dram_tensor("v_scratch", [tokens, half_width], F32).ap()
    ya = nc.dram_tensor("ya_scratch", [tokens, half_width], F32).ap()
    x1 = nc.dram_tensor("x1_scratch", [tokens, width], F32).ap()
    x2 = nc.dram_tensor("x2_scratch", [tokens, width], F32).ap()
    hm = nc.dram_tensor("hm_scratch", [tokens, width], F32).ap()
    ybuf = nc.dram_tensor("y_scratch", [n_blocks * P, width], F32).ap()
    with ExitStack() as stack:
        s = Scope(nc, stack, "all")
        ident, half = s.sbuf("ident", [P, P]), s.sbuf("half", [P, 8])
        gates = s.sbuf("gates", [P, top_k, tiles])
        dests = s.sbuf("dests", [P, top_k, tiles], I32)
        slot_tokens = s.sbuf("slot_tokens", [P, n_blocks + 1], I32)
        block_end = s.sbuf("block_end", [P, experts], I32)
        block_expert = s.sbuf("block_expert", [P, n_blocks + 1], I32)
        block_kind = s.sbuf("block_kind", [P, n_blocks + 1], I32)
        with ExitStack() as before_moe:
            b = Scope(nc, before_moe, "pre")
            logits = b.sbuf("logits", [P, tiles, n_group + experts])
            with ExitStack() as mixing:
                m = Scope(nc, mixing, "mix")
                ident_bf, above = m.sbuf("ident_bf", [P, P], BF16), m.sbuf("above", [P, P], BF16)
                set_constants(nc, ident, half, ident_bf, above)
                project_qkv(nc, x[0], norm_mix[0], w_in[0], ident[:], half, qt, kt, v)
                mix_chunks(nc, x[0], norm_mix[0], w_in[0], v_norm[0], w_spatial[0], b_spatial[0], out_norm_a[0], ident[:], half, ya)
                yb = m.sbuf("yb", [P, tiles, half_width])
                attend_stick(nc, qt, kt, v, ident[:], ident_bf[:], above[:], yb,
                         ybuf[experts * P:, :])
                project_out(nc, ya, yb, out_norm_b[0], w_out[0], x[0], ident[:], half, x1)
            key_t, value = b.sbuf("key_t", [P, rows, slots]), b.sbuf("value", [P, slots // P, width])
            project_memory(nc, mem[0], norm_mem[0], w_xk[0], w_xv[0], ident[:], half, key_t, value)
            attend_memory(nc, x1, norm_cross[0], w_xq[0], w_xo[0], key_t, value, norm_moe[0], w_group[0], w_router[0],
                          b_group[0], b_router[0], ident[:], half, x2, hm, logits)
            route(nc, logits, n_group, gates, dests, slot_tokens, block_end, block_expert, block_kind)
        run_experts(nc, hm, w1[0], w3[0], w2[0], slot_tokens, block_end, block_expert, block_kind, n_blocks, ident[:], ybuf)
        combine(nc, x2, ybuf, gates, dests, norm_final, half, out[0])


_INS = ["x", "mem", "norm_mix", "w_in", "v_norm", "w_spatial", "b_spatial", "out_norm_a", "out_norm_b", "w_out", "norm_cross",
        "norm_mem", "w_xq", "w_xk", "w_xv", "w_xo", "norm_moe", "w_group", "b_group", "w_router", "b_router", "w1", "w3", "w2",
        "norm_final"]


def kernel(**inputs):
    import concourse.bacc as bacc
    from concourse.bass_utils import run_bass_kernel_spmd

    nc = bacc.Bacc("TRN2", target_bir_lowering=False, num_devices=1)
    arrays, args = {}, []
    for name in _INS:
        a = np.ascontiguousarray(inputs[name])
        arrays[f"in_{name}"] = a
        args.append(nc.dram_tensor(f"in_{name}", a.shape, mybir.dt.from_np(a.dtype), kind="ExternalInput").ap())
    out = nc.dram_tensor("out_x", arrays["in_x"].shape, F32, kind="ExternalOutput").ap()
    build_trunk(nc, *args, out)
    got = run_bass_kernel_spmd(nc, [arrays], core_ids=[0])
    return got.results[0]["out_x"]
```
